# Optimizing a Trainium2 kernel written in Bass

```python
import math
import jax, jax.numpy as jnp
from jax import lax
import numpy as np

D_MODEL = 1024
BATCH = 1
SEQ = 256
DEPTH = 2

CTX_LEN = 256
GRID_W = 64
W_FOURIER = D_MODEL // 2
N_FOURIER_GROUPS = 4
W_SSM = D_MODEL // 2
SSM_GROUP = 16
N_SSM_GROUPS = W_SSM // SSM_GROUP
SSM_STATE = 64
DT_MIN = 1e-3
DT_MAX = 1e-1
D_FF = ((8 * D_MODEL // 3 + 255) // 256) * 256
N_EXPERTS = 8
TOP_K = 2
D_FF_EXPERT = 7 * D_MODEL // 2
N_DENSE = (DEPTH + 1) // 2
N_MOE = DEPTH // 2
OFF_SSM = W_FOURIER
OFF_GA = W_FOURIER + W_SSM
OFF_GB = OFF_GA + D_MODEL
IN_COLS = OFF_GB + D_MODEL
EPS = 1e-6
POS_BASE = 10000.0

kernel_name = 'fourier_s5_gated_moe_diffusion_block'

def rmsnorm(x, g):
    xf = x.astype(jnp.float32)
    y = xf * lax.rsqrt(jnp.mean(xf * xf, axis=-1, keepdims=True) + EPS)
    return (y * g.astype(jnp.float32)).astype(x.dtype)

def sincos_2d(rows, dim, dtype):
    t = jnp.arange(rows * GRID_W)
    r = (t // GRID_W).astype(jnp.float32)
    col = (t % GRID_W).astype(jnp.float32)
    quarter = dim // 4
    omega = 1.0 / (POS_BASE ** (jnp.arange(quarter, dtype=jnp.float32) / quarter))
    ar = r[:, None] * omega
    ac = col[:, None] * omega
    return jnp.concatenate([jnp.sin(ar), jnp.cos(ar), jnp.sin(ac), jnp.cos(ac)], axis=-1).astype(dtype)

def adaln(cond, w_mod, b_mod):
    return jnp.split(jax.nn.silu(cond) @ w_mod + b_mod, 6, axis=-1)

def fourier_mix(u):
    b, n, _ = u.shape
    ug = u.reshape(b, n, N_FOURIER_GROUPS, W_FOURIER // N_FOURIER_GROUPS).astype(jnp.float32)
    y = jnp.fft.fft2(ug, axes=(1, 3), norm='ortho').real
    return y.reshape(b, n, W_FOURIER).astype(u.dtype)

def zoh_discretise(a_re, a_im, log_dt, b_re, b_im):
    lam = lax.complex(a_re.astype(jnp.float32), a_im.astype(jnp.float32))
    dt = jnp.exp(log_dt.astype(jnp.float32))[:, None]
    lam_dt = lam * dt
    lam_bar = jnp.exp(lam_dt)
    b_mat = lax.complex(b_re.astype(jnp.float32), b_im.astype(jnp.float32))
    b_bar = ((lam_bar - 1.0) / lam)[..., None] * b_mat
    return lam_dt, lam_bar, b_bar

def _scan_op(e1, e2):
    a1, b1 = e1
    a2, b2 = e2
    return a1 * a2, a2 * b1 + b2

def diag_scan(bu, lam_bar, lam_dt, h0):
    n = bu.shape[1]
    a = jnp.broadcast_to(lam_bar, bu.shape)
    _, h = lax.associative_scan(_scan_op, (a, bu), axis=1)
    if h0 is not None:
        steps = jnp.arange(1, n + 1, dtype=jnp.float32)[:, None, None]
        h = h + jnp.exp(lam_dt[None] * steps)[None] * h0[:, None]
    return h

def s5_branch(u_ctx, u_lat, a_re, a_im, log_dt, b_re, b_im, c_re, c_im, d_skip, need_ctx):
    dtype = u_lat.dtype

    def groups(u):
        return u.reshape(u.shape[0], u.shape[1], N_SSM_GROUPS, SSM_GROUP).astype(jnp.float32)

    uc = groups(u_ctx)
    ul = groups(u_lat)
    d = d_skip.astype(jnp.float32).reshape(N_SSM_GROUPS, SSM_GROUP)
    y_lat = d * ul
    y_ctx = d * uc
    for direction in range(2):
        rev = direction == 1
        flip = (lambda t: jnp.flip(t, axis=1)) if rev else (lambda t: t)
        lam_dt, lam_bar, b_bar = zoh_discretise(a_re[direction], a_im[direction], log_dt[direction],
                                                b_re[direction], b_im[direction])
        c_mat = lax.complex(c_re[direction].astype(jnp.float32), c_im[direction].astype(jnp.float32))
        bu_c = jnp.einsum('blgh,gph->blgp', flip(uc).astype(jnp.complex64), b_bar)
        h_c = diag_scan(bu_c, lam_bar, lam_dt, None)
        bu_l = jnp.einsum('blgh,gph->blgp', flip(ul).astype(jnp.complex64), b_bar)
        h_l = diag_scan(bu_l, lam_bar, lam_dt, h_c[:, -1])
        y_lat = y_lat + flip(jnp.einsum('blgp,ghp->blgh', h_l, c_mat).real)
        if need_ctx:
            y_ctx = y_ctx + flip(jnp.einsum('blgp,ghp->blgh', h_c, c_mat).real)

    def finish(y):
        return jax.nn.gelu(y).reshape(y.shape[0], y.shape[1], W_SSM).astype(dtype)

    return (finish(y_ctx) if need_ctx else None), finish(y_lat)

def merge_branches(p, y_s, w_four, w_glu_a, w_glu_b, w_out):
    g_a = jax.nn.sigmoid(p[..., OFF_GA:OFF_GB])
    g_b = jax.nn.sigmoid(p[..., OFF_GB:])
    y_a = fourier_mix(p[..., :OFF_SSM]) @ w_four
    y_b = (y_s @ w_glu_a) * jax.nn.sigmoid(y_s @ w_glu_b)
    return (g_a * y_a + g_b * y_b) @ w_out

def token_mixer(a_ctx, a_lat, w_in, w_four, a_re, a_im, log_dt, b_re, b_im, c_re, c_im,
                d_skip, w_glu_a, w_glu_b, w_out, need_ctx):
    p_lat = a_lat @ w_in
    if need_ctx:
        p_ctx = a_ctx @ w_in
        s_ctx = p_ctx[..., OFF_SSM:OFF_GA]
    else:
        p_ctx = None
        s_ctx = a_ctx @ w_in[:, OFF_SSM:OFF_GA]
    y_ctx, y_lat = s5_branch(s_ctx, p_lat[..., OFF_SSM:OFF_GA], a_re, a_im, log_dt,
                             b_re, b_im, c_re, c_im, d_skip, need_ctx)
    out_lat = merge_branches(p_lat, y_lat, w_four, w_glu_a, w_glu_b, w_out)
    out_ctx = merge_branches(p_ctx, y_ctx, w_four, w_glu_a, w_glu_b, w_out) if need_ctx else None
    return out_ctx, out_lat

def swiglu(t, w_gate, w_up, w_down):
    return (jax.nn.silu(t @ w_gate) * (t @ w_up)) @ w_down

def moe_swiglu(t, w_router, b_router, w_gate, w_up, w_down):
    b, n, d = t.shape
    tok = t.reshape(b * n, d)
    logits = (tok @ w_router).astype(jnp.float32) + b_router.astype(jnp.float32)
    top_v, top_i = lax.top_k(logits, TOP_K)
    top_w = jax.nn.softmax(top_v, axis=-1)
    combine = jnp.sum(jax.nn.one_hot(top_i, N_EXPERTS, dtype=jnp.float32) * top_w[..., None], axis=1)
    combine = combine.astype(tok.dtype)
    out = jnp.zeros_like(tok)
    for e in range(N_EXPERTS):
        out = out + combine[:, e:e + 1] * swiglu(tok, w_gate[e], w_up[e], w_down[e])
    return out.reshape(b, n, d)

def channel_mixer(l, t, ffn_w_gate, ffn_w_up, ffn_w_down,
                  moe_w_router, moe_b_router, moe_w_gate, moe_w_up, moe_w_down):
    i = l // 2
    if l % 2 == 0:
        return swiglu(t, ffn_w_gate[i], ffn_w_up[i], ffn_w_down[i])
    return moe_swiglu(t, moe_w_router[i], moe_b_router[i], moe_w_gate[i], moe_w_up[i], moe_w_down[i])

def setup_inputs(seed: int = 0) -> dict:
    key = jax.random.key(seed)
    ks = jax.random.split(key, 32)
    f32 = jnp.float32

    def nrm(k, shape, scale):
        return scale * jax.random.normal(k, shape, f32)

    G, P, H = N_SSM_GROUPS, SSM_STATE, SSM_GROUP
    a_im_init = math.pi * jnp.arange(P, dtype=f32)
    return {
        'x': nrm(ks[0], (BATCH, SEQ, D_MODEL), 1.0),
        'c': nrm(ks[1], (BATCH, D_MODEL), 1.0),
        'ctx': nrm(ks[2], (BATCH, CTX_LEN, D_MODEL), 1.0),
        'c_ctx': nrm(ks[3], (D_MODEL,), 1.0),
        'w_mod': nrm(ks[4], (DEPTH, D_MODEL, 6 * D_MODEL), 0.5 * D_MODEL ** -0.5),
        'b_mod': nrm(ks[5], (DEPTH, 6 * D_MODEL), 0.02),
        'norm1_g': 1.0 + nrm(ks[6], (DEPTH, D_MODEL), 0.02),
        'norm2_g': 1.0 + nrm(ks[7], (DEPTH, D_MODEL), 0.02),
        'w_in': nrm(ks[8], (DEPTH, D_MODEL, IN_COLS), D_MODEL ** -0.5),
        'w_four': nrm(ks[9], (DEPTH, W_FOURIER, D_MODEL), W_FOURIER ** -0.5),
        'ssm_a_re': -0.5 + nrm(ks[10], (DEPTH, 2, G, P), 0.01),
        'ssm_a_im': a_im_init + nrm(ks[11], (DEPTH, 2, G, P), 0.01),
        'ssm_log_dt': jax.random.uniform(ks[12], (DEPTH, 2, G), f32, math.log(DT_MIN), math.log(DT_MAX)),
        'ssm_b_re': nrm(ks[13], (DEPTH, 2, G, P, H), (2 * H) ** -0.5),
        'ssm_b_im': nrm(ks[14], (DEPTH, 2, G, P, H), (2 * H) ** -0.5),
        'ssm_c_re': nrm(ks[15], (DEPTH, 2, G, H, P), (2 * P) ** -0.5),
        'ssm_c_im': nrm(ks[16], (DEPTH, 2, G, H, P), (2 * P) ** -0.5),
        'ssm_d': nrm(ks[17], (DEPTH, W_SSM), 1.0),
        'w_glu_a': nrm(ks[18], (DEPTH, W_SSM, D_MODEL), W_SSM ** -0.5),
        'w_glu_b': nrm(ks[19], (DEPTH, W_SSM, D_MODEL), W_SSM ** -0.5),
        'w_out': nrm(ks[20], (DEPTH, D_MODEL, D_MODEL), D_MODEL ** -0.5),
        'ffn_w_gate': nrm(ks[21], (N_DENSE, D_MODEL, D_FF), D_MODEL ** -0.5),
        'ffn_w_up': nrm(ks[22], (N_DENSE, D_MODEL, D_FF), D_MODEL ** -0.5),
        'ffn_w_down': nrm(ks[23], (N_DENSE, D_FF, D_MODEL), D_FF ** -0.5),
        'moe_w_router': nrm(ks[24], (N_MOE, D_MODEL, N_EXPERTS), D_MODEL ** -0.5),
        'moe_b_router': nrm(ks[25], (N_MOE, N_EXPERTS), 0.01),
        'moe_w_gate': nrm(ks[26], (N_MOE, N_EXPERTS, D_MODEL, D_FF_EXPERT), D_MODEL ** -0.5),
        'moe_w_up': nrm(ks[27], (N_MOE, N_EXPERTS, D_MODEL, D_FF_EXPERT), D_MODEL ** -0.5),
        'moe_w_down': nrm(ks[28], (N_MOE, N_EXPERTS, D_FF_EXPERT, D_MODEL), D_FF_EXPERT ** -0.5),
        'final_g': 1.0 + nrm(ks[29], (D_MODEL,), 0.02),
    }

def reference(x, c, ctx, c_ctx, w_mod, b_mod, norm1_g, norm2_g, w_in, w_four,
              ssm_a_re, ssm_a_im, ssm_log_dt, ssm_b_re, ssm_b_im, ssm_c_re, ssm_c_im, ssm_d,
              w_glu_a, w_glu_b, w_out, ffn_w_gate, ffn_w_up, ffn_w_down,
              moe_w_router, moe_b_router, moe_w_gate, moe_w_up, moe_w_down, final_g):
    rows = x.shape[1] // GRID_W
    h = x + sincos_2d(rows, D_MODEL, x.dtype)[None]
    z = ctx
    for l in range(DEPTH):
        need_ctx = l < DEPTH - 1
        sh1, sc1, g1, sh2, sc2, g2 = [m[:, None, :] for m in adaln(c, w_mod[l], b_mod[l])]
        csh1, csc1, cg1, csh2, csc2, cg2 = adaln(c_ctx, w_mod[l], b_mod[l])
        a_lat = rmsnorm(h, norm1_g[l]) * (1.0 + sc1) + sh1
        a_ctx = rmsnorm(z, norm1_g[l]) * (1.0 + csc1) + csh1
        o_ctx, o_lat = token_mixer(a_ctx, a_lat, w_in[l], w_four[l],
                                   ssm_a_re[l], ssm_a_im[l], ssm_log_dt[l],
                                   ssm_b_re[l], ssm_b_im[l], ssm_c_re[l], ssm_c_im[l], ssm_d[l],
                                   w_glu_a[l], w_glu_b[l], w_out[l], need_ctx)
        h = h + g1 * o_lat
        f_lat = rmsnorm(h, norm2_g[l]) * (1.0 + sc2) + sh2
        h = h + g2 * channel_mixer(l, f_lat, ffn_w_gate, ffn_w_up, ffn_w_down,
                                   moe_w_router, moe_b_router, moe_w_gate, moe_w_up, moe_w_down)
        if need_ctx:
            z = z + cg1 * o_ctx
            f_ctx = rmsnorm(z, norm2_g[l]) * (1.0 + csc2) + csh2
            z = z + cg2 * channel_mixer(l, f_ctx, ffn_w_gate, ffn_w_up, ffn_w_down,
                                        moe_w_router, moe_b_router, moe_w_gate, moe_w_up, moe_w_down)
    return rmsnorm(h, final_g)


_drawn_inputs = setup_inputs


def setup_inputs(seed=0):
    import zlib

    import numpy as np

    out = dict(_drawn_inputs(seed))
    spreads = {}
    factors = {'ctx': 64.0,
     'c_ctx': 64.0,
     'norm1_g': 8.0,
     'norm2_g': 3.573,
     'ssm_a_re': 64.0,
     'ssm_a_im': 43.576,
     'ssm_log_dt': 46.744,
     'ssm_b_re': 46.864,
     'ssm_b_im': 42.56,
     'ssm_c_re': 59.64,
     'ssm_c_im': 46.112,
     'moe_b_router': 4.614,
     'final_g': 8.531}
    for name, (base, spread) in spreads.items():
        noise = np.random.default_rng([zlib.crc32(name.encode()), seed]).standard_normal(out[name].shape)
        drawn = base * np.exp(spread * noise) if base else spread * noise
        out[name] = __import__('jax').numpy.asarray(drawn.astype(out[name].dtype))
    for name, factor in factors.items():
        out[name] = (out[name] * factor).astype(out[name].dtype)
    return out
```

```python
from contextlib import ExitStack

import numpy as np
import concourse.bass as bass
from concourse import mybir

F32 = mybir.dt.float32
I32 = mybir.dt.int32
U32 = mybir.dt.uint32
ALU = mybir.AluOpType
ACT = mybir.ActivationFunctionType
AX = mybir.AxisListType

P = 128
D = 1024
KD = D // P
CTX = 256
SEQ = 256
NT = CTX + SEQ
DEPTH = 2
WF = 512
MB = WF // P
CHUNK = 4
NCH = NT // CHUNK
ST = 64
SG = 16
FF = 2816
FB = FF // P
NE = 8
FE = 3584
FCH = FE // 512
EPS = 1e-6
RING = 3
MRING = 7
SLOT = 4096
NK = CHUNK + 1
TAB = (NK + 1) * 2 * ST
CPW = 4 * CHUNK * P
CKW = CPW + (2 * CHUNK - 1) * P
ADA_TILES = 12 * DEPTH

C_ID, C_ONE, C_TRI, C_BLK, C_IOTA = 0, 128, 256, 384, 512
C_CS, C_CN, C_SN, C_MG, C_MZ, C_SEL = 768, 1024, 1536, 2048, 2050, 2052
C_N = 2054


def constants():
    c = np.zeros((P, C_N), np.float32)
    p = np.arange(P)
    c[:, C_ID:C_ID + P] = np.eye(P)
    c[:, C_ONE:C_ONE + P] = 1.0
    c[:, C_TRI:C_TRI + P] = p[:, None] < p[None, :]
    c[:, C_BLK:C_BLK + P] = (p[:, None] // SG) == (p[None, :] // SG)
    c[:, C_IOTA:C_IOTA + 256] = np.arange(256)
    a = 2 * np.pi * np.outer(p, p) / P
    s = 1.0 / np.sqrt(float(SEQ * P))
    c[:, C_CS:C_CS + P] = np.cos(a) * s
    c[:, C_CS + P:C_CS + 2 * P] = np.sin(a) * s
    t = np.arange(SEQ)
    b = 2 * np.pi * (np.outer(t, t) % SEQ) / SEQ
    c[:, C_CN:C_CN + 512] = np.cos(b).reshape(2, P, SEQ).transpose(1, 0, 2).reshape(P, 512)
    c[:, C_SN:C_SN + 512] = -np.sin(b).reshape(2, P, SEQ).transpose(1, 0, 2).reshape(P, 512)
    for j in range(2):
        c[:, C_MG + j] = (p // SG) % 2 == j
        c[:, C_MZ + j] = p % 2 == j
        c[:, C_SEL + j] = p % 32 == j
    return c


def positions():
    t = np.arange(SEQ)
    q = D // 4
    omega = (1.0 / (np.float32(10000.0) ** (np.arange(q, dtype=np.float32) / np.float32(q)))).astype(np.float32)
    ar = (t // 64).astype(np.float32)[:, None] * omega
    ac = (t % 64).astype(np.float32)[:, None] * omega
    e = np.concatenate([np.sin(ar), np.cos(ar), np.sin(ac), np.cos(ac)], axis=-1).astype(np.float32)
    return np.ascontiguousarray(e.T.reshape(KD, P, SEQ).transpose(1, 0, 2))


def program(nc, a, out, tab, bps, cks):
    top = ExitStack()
    with top:
        def sem(name):
            return top.enter_context(nc.semaphore(name))

        def sb(stack, name, shape, dt=F32):
            return stack.enter_context(nc.sbuf_tensor(name, shape, dt))

        ps = top.enter_context(nc.psum_tensor("ps", [P, 8, 512], F32))

        con = sb(top, "con", [P, C_N])
        hT = sb(top, "hT", [P, KD, NT])
        aT = sb(top, "aT", [P, KD, NT])
        modv = sb(top, "modv", [P, DEPTH, 48, 2])
        bmod = sb(top, "bmod", [P, DEPTH, 48])
        gains = sb(top, "gains", [P, 5, KD])
        nsc = sb(top, "nsc", [P, 4, KD, 2])
        rms = sb(top, "rms", [P, NT])
        epst = sb(top, "epst", [P, 1])
        L8 = sb(top, "L8", [P, 3, DEPTH * 32])
        wrt = sb(top, "wrt", [P, KD, NE])
        brt = sb(top, "brt", [P, NE])
        dskip = sb(top, "dskip", [P, DEPTH, MB])
        modf = modv[:].rearrange("p l a c -> p (l a) c")
        bmodf = bmod[:].rearrange("p l a -> p (l a)")
        ident = con[:, C_ID:C_ID + P]
        ones = con[:, C_ONE:C_ONE + P]

        inputs_in = sem("inputs_in")
        params_in = sem("params_in")
        landed = [sem(f"landed{i}") for i in range(RING)]
        dve_step = sem("dve_step")
        act_step = sem("act_step")
        silu_c_ready = sem("silu_c_ready")
        tab_ready = sem("tab_ready")
        tab_stored = sem("tab_stored")
        xl_in = [sem(f"xl_in{i}") for i in range(2)]
        bp_free = sem("bp_free")
        cp_free = sem("cp_free")
        kb_free = sem("kb_free")
        mod_bank_zero = sem("mod_bank_zero")
        mod_rows_done = sem("mod_rows_done")
        mod_rows_taken = sem("mod_rows_taken")
        mod_cols_done = sem("mod_cols_done")
        mod_cols_taken = sem("mod_cols_taken")
        bp_made = sem("bp_made")
        bp_masked = sem("bp_masked")
        cp_made = sem("cp_made")
        cp_masked = sem("cp_masked")
        tr_done = sem("tr_done")
        tr_taken = sem("tr_taken")
        taps_done = sem("taps_done")
        kb_made = sem("kb_made")
        l8_done = sem("l8_done")
        l8_masked = sem("l8_masked")
        sq_ready = sem("sq_ready")
        root_ready = sem("root_ready")
        a_ready = sem("a_ready")
        dense_done = sem("dense_done")
        dense_free = [sem(f"dense_free{i}") for i in range(4)]
        side_done = sem("side_done")
        side_free = [sem(f"side_free{i}") for i in range(4)]
        scan_step = sem("scan_step")
        ys_ready = sem("ys_ready")
        mix_ready = sem("mix_ready")
        out_ready = sem("out_ready")
        out_stored = sem("out_stored")

        dense_order, side_order = [], []
        for l in range(DEPTH):
            dense_order += [("ss", l, 0)]
            dense_order += [("u", l, m) for m in range(4)] + [("f", l, m) for m in range(4)]
            for n in ("ga", "gb", "ya", "glub", "glua", "out"):
                dense_order += [(n, l, m) for m in range(8)]
            dense_order += [("ss", l, 1)]
            if l == 0:
                for m in range(FB):
                    dense_order += [("gate", l, m), ("up", l, m)]
                dense_order += [("down", l, m) for m in range(8)]
            side_order += [("E", l, m, g) for m in range(4) for g in range(4)]
            side_order += [("dft1", l, m, t) for m in range(4) for t in range(2 * l, 4)]
            side_order += [("dft2", l, m, s) for m in range(4) for s in range(l, 2)]
            side_order += [("Y", l, m) for m in range(4)]
        dense_at = {k: i for i, k in enumerate(dense_order)}
        side_at = {k: i for i, k in enumerate(side_order)}

        def place(key):
            if key in dense_at:
                i = dense_at[key]
                return ps[:, i % 4, :], dense_done, dense_free[i % 4], i
            i = side_at[key]
            return ps[:, 4 + i % 4, :], side_done, side_free[i % 4], i

        def bank_for(pe, key):
            bank, _, free, i = place(key)
            if i >= 4:
                pe.wait_ge(free, i // 4)
            return bank

        def arrived(eng, key):
            bank, done, free, i = place(key)
            eng.wait_ge(done, i + 1)
            return bank, free

        def taken(eng, key):
            _, _, free, i = place(key)
            eng.wait_ge(free, i // 4 + 1)

        stream = []
        for l in range(DEPTH):
            stream += [("w_in", l, 1), ("w_in", l, 0)]
            stream += [("bp", l, h) for h in range(2)]
            stream += [("w_in", l, n) for n in (2, 3, 4, 5)]
            stream += [("w_four", l, 0)]
            stream += [("ck", l, m) for m in range(4)]
            stream += [("w_glu_b", l, 0), ("w_glu_a", l, 0), ("w_out", l, 0), ("w_out", l, 1)]
            if l == 0:
                stream += [("ffn_gu", l, n) for n in range(FB // 2)]
                stream += [("ffn_down", l, n) for n in range(8)]
        ADA = 12 * DEPTH
        stream_at = {k: ADA + i for i, k in enumerate(stream)}

        last_use = {}
        for l in range(DEPTH):
            last_use.update({("w_in", l, 1): ("u", l, 3), ("w_in", l, 0): ("f", l, 3),
                             ("w_in", l, 2): ("ga", l, 3), ("w_in", l, 3): ("ga", l, 7),
                             ("w_in", l, 4): ("gb", l, 3), ("w_in", l, 5): ("gb", l, 7),
                             ("w_four", l, 0): ("ya", l, 7), ("w_glu_b", l, 0): ("glub", l, 7),
                             ("w_glu_a", l, 0): ("glua", l, 7), ("w_out", l, 0): ("out", l, 3),
                             ("w_out", l, 1): ("out", l, 7)})
            last_use.update({("bp", l, h): ("E", l, 2 * h + 1, 3) for h in range(2)})
            last_use.update({("ck", l, m): ("Y", l, m) for m in range(4)})
            for n in range(FB // 2):
                last_use[("ffn_gu", l, n)] = ("up", l, 2 * n + 1)
            for n in range(8):
                last_use[("ffn_down", l, n)] = ("down", l, 2 * (n // 2) + 1)

        moe_order = [("gate", 0), ("up", 0)]
        for c in range(1, FCH):
            moe_order += [("gate", c), ("up", c), ("down", c - 1)]
        moe_order += [("down", FCH - 1)]
        moe_at = {k: i for i, k in enumerate(moe_order)}

        def tile_src(key):
            n, l, i = key
            if n in ("w_in", "w_out"):
                return a[n][l, i]
            if n in ("w_four", "w_glu_a", "w_glu_b"):
                return a[n][l]
            if n in ("ffn_gu", "ffn_down"):
                return a[n][i]
            if n == "bp":
                return bps[4 * l + 2 * i:4 * l + 2 * i + 2].rearrange("m p c -> p m c")
            return cks[l * 4 + i]

        early = ExitStack()
        ring = [sb(early, f"ring{i}", [P, SLOT]) for i in range(RING)]
        silu_c = sb(early, "silu_c", [P, KD, 2])

        par = ExitStack()
        zt = sb(par, "zt", [P, NK + 1, 2, ST])
        zi = sb(par, "zi", [P, 2, ST])
        ldt = sb(par, "ldt", [P, 1])
        zs = sb(par, "zs", [P, 14, ST])
        zint = sb(par, "zint", [P, ST], I32)
        l8m = sb(par, "l8m", [P, 2, 2, ST])
        XLs = [sb(par, f"XL{i}", [P, 2, NK + 1, 2, ST]) for i in range(2)]
        BCs = [sb(par, f"BC{i}", [P, 2, 2, 2, ST]) for i in range(2)]
        mrow = sb(par, "mrow", [P, 2, 512])
        Bb = sb(par, "Bb", [P, 2, 2, ST])
        t1 = sb(par, "t1", [P, NK, ST])
        t2 = sb(par, "t2", [P, NK, ST])
        t3 = sb(par, "t3", [P, NK, ST])
        t4 = sb(par, "t4", [P, NK, ST])
        BP = sb(par, "BP", [P, 2, 2, CHUNK, ST])
        BPm = sb(par, "BPm", [P, 2, 2, CHUNK, 2, ST])
        CP = sb(par, "CP", [P, 2, 2, NK, ST])
        CPm = sb(par, "CPm", [P, 2, 2, NK, 2, ST])
        CTr = sb(par, "CTr", [P, 2 * 2 * NK + 4, P])
        KB = sb(par, "KB", [P, 2 * CHUNK, P])
        par.close()

        mid = ExitStack()
        R1 = sb(mid, "R1", [P, 3 * SLOT])
        G = R1[:, 0:SLOT].rearrange("p (k t) -> p k t", k=KD)
        G2 = R1[:, SLOT:2 * SLOT].rearrange("p (k t) -> p k t", k=KD)
        Q = R1[:, 2 * SLOT:3 * SLOT].rearrange("p (a m c) -> p a m c", a=4, m=4)
        ysT = R1[:, 2 * SLOT:2 * SLOT + MB * NT].rearrange("p (m t) -> p m t", m=MB)
        hid = R1[:, 0:FB * NT].rearrange("p (k t) -> p k t", k=FB)
        uT = sb(mid, "uT", [P, MB, NT])
        uF = sb(mid, "uF", [P, MB, NT])
        ypre = sb(mid, "ypre", [P, 2, NT])
        H = sb(mid, "H", [P, NCH + 1, 2, 32])
        sc1 = sb(mid, "sc1", [P, 2, 32])
        sc2 = sb(mid, "sc2", [P, 2, 32])
        sg = sb(mid, "sg", [P, 2, NT])
        mid.close()
        early.close()

        moe = ExitStack()
        mring = [sb(moe, f"mring{i}", [P, SLOT]) for i in range(MRING)]
        ftok = sb(moe, "ftok", [P, 2, D])
        lg = sb(moe, "lg", [P, 2, NE])
        mx = sb(moe, "mx", [P, 2, 8])
        mi = sb(moe, "mi", [P, 2, 8], U32)
        mif = sb(moe, "mif", [P, 2, 8])
        wt = sb(moe, "wt", [P, 2, 4])
        oh = sb(moe, "oh", [P, 2, 2, NE])
        sel = sb(moe, "sel", [P, 2, NE])
        comb = sb(moe, "comb", [P, 2, NE])
        rank = sb(moe, "rank", [P, 2, NE])
        cnt = sb(moe, "cnt", [P, 1])
        cnti = sb(moe, "cnti", [P, 1], I32)
        S = sb(moe, "S", [P, 2, P])
        SW = sb(moe, "SW", [P, 2, P])
        SWT = sb(moe, "SWT", [P, SEQ])
        XG = sb(moe, "XG", [P, KD, P])
        gs = sb(moe, "gs", [P, 2, 512])
        hd = sb(moe, "hd", [P, 2, 512])
        hTc = sb(moe, "hTc", [P, 2, 4, P])
        ye = sb(moe, "ye", [P, D])
        moe.close()

        mlanded = [sem(f"mlanded{i}") for i in range(MRING)]
        down_done = sem("down_done")
        logits_done = sem("logits_done")
        weights_exp = sem("weights_exp")
        top_ready = sem("top_ready")
        sel_ready = sem("sel_ready")
        rank_done = sem("rank_done")
        rank_ready = sem("rank_ready")
        count_ready = sem("count_ready")
        ftok_done = sem("ftok_done")
        ftok_ready = sem("ftok_ready")
        onehot_ready = sem("onehot_ready")
        misc_done = sem("misc_done")
        misc_taken = [sem(f"misc_taken{i}") for i in range(2)]
        gateup_done = sem("gateup_done")
        gate_taken = sem("gate_taken")
        hid_ready = sem("hid_ready")
        ye_ready = sem("ye_ready")
        fin_done = sem("fin_done")

        block = top.enter_context(nc.Block())
        MISC = 2 + 1 + FCH + 4

        @block.sync
        def _(sp):
            sp.dma_start(con[:, :], a["con"]).then_inc(inputs_in, 16)
            for t, n in ((bmod, "bmod"), (gains, "gains"), (dskip, "dskip"), (wrt, "wrt"), (brt, "brt")):
                sp.dma_start(t[:], a[n]).then_inc(inputs_in, 16)
            sp.dma_start(silu_c[:], a["cT"]).then_inc(inputs_in, 16)
            for j in range(RING):
                sp.dma_start(ring[j][:], a["w_mod"][j]).then_inc(landed[j], 16)
            with sp.Fori(1, ADA // RING) as i:
                for j in range(RING):
                    sp.wait_ge(mod_rows_done, i * RING + (j + 1 - RING))
                    sp.dma_start(ring[j][:], a["w_mod"][bass.ds(i * RING + j, 1), :, :]
                                 .rearrange("o p c -> p (o c)")).then_inc(landed[j], 16)
            for key in stream:
                n = stream_at[key]
                if key[0] == "bp" or key[0] == "ck":
                    for s_ in (bp_free,) if key[0] == "bp" else (cp_free, kb_free):
                        sp.wait_ge(s_, 16 * (2 * MB + 1))
                if n - RING < ADA:
                    sp.wait_ge(mod_rows_done, n - RING + 1)
                else:
                    _, done, _, at = place(last_use[stream[n - RING - ADA]])
                    sp.wait_ge(done, at + 1)
                src = tile_src(key)
                dst = ring[n % RING][:, 0:src.shape[-1]]
                if key[0] == "bp":
                    dst = ring[n % RING][:].rearrange("p (m c) -> p m c", m=2)
                sp.dma_start(dst, src).then_inc(landed[n % RING], 16)

            def expert(e, x, first=False):
                for t, (kind, c) in enumerate(moe_order):
                    if not (first and t < MRING):
                        k, cc = moe_order[(t - MRING) % len(moe_order)]
                        y = x - 1 if t < MRING else x
                        if k == "down":
                            sp.wait_ge(down_done, y * FCH + (cc + 1))
                        else:
                            sp.wait_ge(gateup_done, y * (2 * FCH) + (2 * cc + 1 + (k == "up")))
                    sp.dma_start(mring[t % MRING][:], a["moe_" + kind][bass.ds(e * FCH + c, 1), :, :]
                                 .rearrange("o p c -> p (o c)")).then_inc(mlanded[t % MRING], 16)

            sp.wait_ge(dense_done, dense_at[("out", DEPTH - 1, 7)] + 1)
            expert(0, 0, first=True)
            with sp.Fori(1, NE) as e:
                expert(e, e)
            sp.wait_ge(count_ready, 1)
            most = sp.value_load(cnti[0:1, 0:1], min_val=0, max_val=SEQ)
            with sp.If(most > P):
                with sp.Fori(0, NE) as e:
                    expert(e, e + NE)
            sp.wait_ge(out_ready, 1)
            sp.dma_start(out, aT[:, :, CTX:NT]).then_inc(out_stored, 16)
            sp.wait_ge(out_stored, 16)

        @block.scalar
        def _(act):
            steps = [0]

            def link(ins):
                steps[0] += 1
                ins.then_inc(act_step, 1)
                act.wait_ge(act_step, steps[0])

            for t, n in ((zi, "lam"), (ldt, "ldt"), (hT, "xT")):
                act.dma_start(t[:], a[n]).then_inc(params_in, 16)
            act.dma_start(aT[:, :, 0:SEQ], a["pos"]).then_inc(params_in, 16)
            act.wait_ge(inputs_in, 7 * 16)
            nc.scalar.activation(silu_c[:], silu_c[:], ACT.Silu).then_inc(silu_c_ready, 1)
            act.wait_ge(tab_ready, 1)
            act.dma_start(tab, zt[:].rearrange("p a b c -> p (a b c)")).then_inc(tab_stored, 16)
            act.wait_ge(tab_stored, 16)
            for s_ in (bp_free, cp_free, kb_free):
                act.sem_inc(s_, 16)

            def load_block(it, h):
                for d in range(2):
                    src = tab[bass.ds(it * 16 + d * 8, 8), :].unsqueeze(1).to_broadcast([8, SG, TAB])
                    act.dma_start(XLs[h][:, d].rearrange("p a b c -> p (a b c)"), src).then_inc(xl_in[h], 16)
                act.dma_start(BCs[h][:].rearrange("p a b c d -> p (a b c d)"),
                              a["bc"][bass.ds(it, 1), :, :].rearrange("o p c -> p (o c)")).then_inc(xl_in[h], 16)

            load_block(0, 0)
            with act.Fori(0, MB) as i:
                for h in range(2):
                    it = i * 2 + h
                    load_block((it + 1) % (2 * MB), 1 - h)
                    for j in range(RING):
                        act.wait_ge(mod_rows_done, it * RING + j + 1)
                        if j >= 2:
                            act.wait_ge(mod_cols_done, it * RING + j - 1)
                        nc.scalar.activation(mrow[:, j % 2, :], ps[:, 6 + j % 2, :], ACT.Copy)\
                            .then_inc(mod_rows_taken, 1)
                    act.wait_ge(bp_made, it + 1)
                    act.wait_ge(bp_free, it * 16 + 16)
                    for b in range(2):
                        nc.scalar.activation(BPm[:].rearrange("p a b k c s -> p (a b k) c s")[:, :, b, :],
                                             BP[:].rearrange("p a b k s -> p (a b k) s"),
                                             ACT.Copy, scale=con[:, C_MG + b:C_MG + b + 1]).then_inc(bp_masked, 1)
                    act.wait_ge(bp_masked, it * 2 + 2)
                    act.dma_start(bps[bass.ds(it, 1), :, :].rearrange("o p c -> p (o c)"),
                                  BPm[:].rearrange("p a b c d e -> p (a b c d e)")).then_inc(bp_free, 16)
                    act.wait_ge(cp_made, it + 1)
                    for b in range(2):
                        nc.scalar.activation(CPm[:].rearrange("p a b k c s -> p (a b k) c s")[:, :, b, :],
                                             CP[:].rearrange("p a b k s -> p (a b k) s"),
                                             ACT.Copy, scale=con[:, C_MG + b:C_MG + b + 1]).then_inc(cp_masked, 1)
                    act.wait_ge(cp_free, it * 16 + 16)
                    for g in range(NK + 1):
                        act.wait_ge(tr_done, it * (NK + 1) + g + 1)
                        nc.scalar.activation(CTr[:, 4 * g:4 * g + 4, :].rearrange("p a c -> p (a c)"),
                                             ps[:, g % 2, :], ACT.Copy).then_inc(tr_taken, 1)
                    act.wait_ge(tr_taken, it * (NK + 1) + (NK + 1))
                    act.dma_start(
                        cks[bass.ds(it, 1), :, 0:CPW].rearrange("o p (a c) -> p (o a) c", a=4),
                        CTr[:, 0:4 * NK, :].rearrange("p (a k) c -> p a (k c)", a=4)[:, :, P:NK * P])\
                        .then_inc(cp_free, 16)
                    act.wait_ge(kb_made, it + 1)
                    act.dma_start(cks[bass.ds(it, 1), :, CPW:CKW].rearrange("o p c -> p (o c)"),
                                  KB[:, 0:2 * CHUNK - 1, :].rearrange("p a c -> p (a c)")).then_inc(kb_free, 16)
            act.wait_ge(xl_in[0], 48 * (MB + 1))
            for s_ in (bp_free, cp_free, kb_free):
                act.wait_ge(s_, 16 * (2 * MB + 1))

            def root(k, l, n):
                bank, free = arrived(act, (k, l, n))
                lo = CTX if (l, n) == (1, 1) else 0
                nc.scalar.activation(rms[:, lo:NT], bank[:, lo:NT], ACT.Sqrt, scale=1.0 / D,
                                     bias=epst[:, 0:1]).then_inc(free, 1)

            def evac(key, dst, func=ACT.Copy, cols=NT):
                bank, free = arrived(act, key)
                nc.scalar.activation(dst, bank[:, 0:cols], func).then_inc(free, 1)

            for l in range(DEPTH):
                t0 = CTX * l
                n = NT - t0
                root("ss", l, 0)
                for m in range(4):
                    evac(("u", l, m), uT[:, m, :])
                for m in range(4):
                    evac(("f", l, m), uF[:, m, t0:NT], cols=n)
                for m in range(4):
                    for t in range(2 * l, 4):
                        evac(("dft1", l, m, t), Q[:, t, m, :], cols=2 * P)
                for m in range(4):
                    for s in range(l, 2):
                        evac(("dft2", l, m, s), uF[:, m, s * 256:s * 256 + 256], cols=256)
                for m in range(8):
                    evac(("ga", l, m), G[:, m, t0:NT], ACT.Sigmoid, n)
                for m in range(8):
                    evac(("gb", l, m), G2[:, m, t0:NT], ACT.Sigmoid, n)
                for m in range(4):
                    act.wait_ge(side_free[side_at[("Y", l, m)] % 4], side_at[("Y", l, m)] // 4 + 1)
                    nc.scalar.activation(ysT[:, m, t0:NT], ypre[:, m % 2, t0:NT],
                                         ACT.Gelu_apprx_tanh).then_inc(ys_ready, 1)
                for m in range(8):
                    evac(("glub", l, m), aT[:, m, t0:NT], ACT.Sigmoid, n)
                root("ss", l, 1)
                if l == 0:
                    for m in range(FB):
                        if m >= 2:
                            taken(act, ("up", l, m - 2))
                        evac(("gate", l, m), sg[:, m % 2, :], ACT.Silu)

            act.wait_ge(top_ready, 1)
            nc.scalar.activation(wt[:, :, 1:2], wt[:, :, 0:1], ACT.Exp).then_inc(weights_exp, 1)
            for g in range(4):
                act.wait_ge(ftok_done, g + 1)
                nc.scalar.activation(ftok[:, g // 2, (g % 2) * 512:(g % 2) * 512 + 512], ps[:, g, :],
                                     ACT.Copy).then_inc(ftok_ready, 1)

            def experts(pas):
                with act.Fori(0, NE) as e:
                    x = e + NE * pas
                    for g in range(2):
                        act.wait_ge(misc_done, x * MISC + g + 1)
                        nc.scalar.activation(XG[:, 4 * g:4 * g + 4, :].rearrange("p a c -> p (a c)"),
                                             ps[:, 6 + g, :], ACT.Copy).then_inc(misc_taken[g], 1)
                    act.wait_ge(misc_done, x * MISC + 3)
                    nc.scalar.activation(SWT[:], ps[:, 6, 0:SEQ], ACT.Copy).then_inc(misc_taken[0], 1)
                    for c in range(FCH + 1):
                        if c < FCH:
                            act.wait_ge(gateup_done, x * 2 * FCH + 2 * c + 1)
                            if c >= 2:
                                act.wait_ge(hid_ready, x * FCH + c - 1)
                            nc.scalar.activation(gs[:, c % 2, :], ps[:, 2 * (c % 2), :], ACT.Silu)\
                                .then_inc(gate_taken, 1)
                        if c >= 1:
                            b = (3 + c - 1) % 2
                            act.wait_ge(misc_done, x * MISC + 3 + c)
                            nc.scalar.activation(hTc[:, (c - 1) % 2].rearrange("p a c -> p (a c)"),
                                                 ps[:, 6 + b, :], ACT.Copy).then_inc(misc_taken[b], 1)
                    act.wait_ge(down_done, x * FCH + FCH)
                    nc.scalar.activation(ye[:, 0:512], ps[:, 4, :], ACT.Copy).then_inc(ye_ready, 1)
                    nc.scalar.activation(ye[:, 512:D], ps[:, 5, :], ACT.Copy).then_inc(ye_ready, 1)
            experts(0)
            act.wait_ge(count_ready, 1)
            most = act.value_load(cnti[0:1, 0:1], min_val=0, max_val=SEQ)
            with act.If(most > P):
                experts(1)
            act.wait_ge(fin_done, 1)
            nc.scalar.activation(rms[:, 0:SEQ], ps[:, 0, 0:SEQ], ACT.Sqrt, scale=1.0 / D,
                                 bias=epst[:, 0:1]).then_inc(root_ready, 1)

        @block.vector
        def _(dve):
            V = nc.vector
            steps = [0]

            def link(ins):
                steps[0] += 1
                ins.then_inc(dve_step, 1)
                dve.wait_ge(dve_step, steps[0])

            link(V.memset(epst[:], EPS))
            dve.wait_ge(params_in, 4 * 16)
            link(V.tensor_tensor(hT[:, :, CTX:NT], hT[:, :, CTX:NT], aT[:, :, 0:SEQ], ALU.add))

            z = [zs[:, k, :] for k in range(14)]
            BIG = 12582912.0

            def exp_to(dst, x, n, r, w, ti, cols):
                c = slice(0, cols)
                link(V.tensor_scalar(n[:, c], x, -87.0, 88.0, ALU.max, ALU.min))
                link(V.tensor_copy(w[:, c], n[:, c]))
                link(V.tensor_scalar(n[:, c], n[:, c], 1.4426950408889634, BIG, ALU.mult, ALU.add))
                link(V.tensor_scalar(n[:, c], n[:, c], BIG, None, ALU.subtract))
                link(V.scalar_tensor_tensor(w[:, c], n[:, c], -0.693359375, w[:, c], ALU.mult, ALU.add))
                link(V.scalar_tensor_tensor(r[:, c], n[:, c], 2.12194440e-4, w[:, c], ALU.mult, ALU.add))
                link(V.tensor_scalar(n[:, c], n[:, c], 127.0, 8388608.0, ALU.add, ALU.mult))
                link(V.tensor_copy(ti[:, c], n[:, c]))
                link(V.tensor_scalar(w[:, c], r[:, c], 1.0 / 5040, None, ALU.mult))
                for k in (720, 120, 24, 6, 2, 1):
                    link(V.scalar_tensor_tensor(w[:, c], w[:, c], 1.0 / k, r[:, c], ALU.add, ALU.mult))
                link(V.tensor_scalar(w[:, c], w[:, c], 1.0, None, ALU.add))
                link(V.tensor_tensor(w[:, c], w[:, c], ti[:, c].bitcast(F32), ALU.mult))
                link(V.tensor_scalar(n[:, c], x, -87.0, None, ALU.is_ge))
                link(V.tensor_tensor(dst, w[:, c], n[:, c], ALU.mult))

            are, aim = zi[:, 0, :], zi[:, 1, :]
            exp_to(z[0][:, 0:1], ldt[:, 0:1], z[1], z[2], z[3], zint, 1)
            dt = z[0][:, 0:1]
            link(V.tensor_scalar(z[4], are, dt, None, ALU.mult))
            link(V.tensor_scalar(z[5], aim, dt, None, ALU.mult))
            exp_to(z[6], z[4], z[1], z[2], z[3], zint, ST)
            n, r, r2, s, c, qa, qb, w = z[1], z[2], z[3], z[7], z[8], z[9], z[10], z[11]
            link(V.tensor_scalar(n, z[5], 0.6366197723675814, BIG, ALU.mult, ALU.add))
            link(V.tensor_scalar(n, n, BIG, None, ALU.subtract))
            link(V.scalar_tensor_tensor(r, n, -1.5703125, z[5], ALU.mult, ALU.add))
            link(V.scalar_tensor_tensor(r, n, -4.837512969970703125e-4, r, ALU.mult, ALU.add))
            link(V.scalar_tensor_tensor(r, n, -7.54978995489188216e-8, r, ALU.mult, ALU.add))
            link(V.tensor_tensor(r2, r, r, ALU.mult))
            link(V.tensor_scalar(s, r2, 1.0 / 362880, None, ALU.mult))
            for k in (-1.0 / 5040, 1.0 / 120, -1.0 / 6):
                link(V.scalar_tensor_tensor(s, s, k, r2, ALU.add, ALU.mult))
            link(V.scalar_tensor_tensor(s, s, 1.0, r, ALU.add, ALU.mult))
            link(V.tensor_scalar(c, r2, -1.0 / 3628800, None, ALU.mult))
            for k in (1.0 / 40320, -1.0 / 720, 1.0 / 24, -0.5):
                link(V.scalar_tensor_tensor(c, c, k, r2, ALU.add, ALU.mult))
            link(V.tensor_scalar(c, c, 1.0, None, ALU.add))
            link(V.tensor_scalar(w, n, 0.25, BIG, ALU.mult, ALU.add))
            link(V.tensor_scalar(w, w, BIG, None, ALU.subtract))
            link(V.scalar_tensor_tensor(n, w, -4.0, n, ALU.mult, ALU.add))
            link(V.tensor_tensor(w, n, n, ALU.mult))
            link(V.tensor_scalar(qb, w, 4.0, None, ALU.is_equal))
            link(V.tensor_scalar(qa, n, 0.0, None, ALU.is_equal))
            link(V.tensor_tensor(qa, qa, qb, ALU.subtract))
            link(V.tensor_scalar(qb, n, 1.0, None, ALU.is_equal))
            link(V.tensor_scalar(w, n, -1.0, None, ALU.is_equal))
            link(V.tensor_tensor(qb, qb, w, ALU.subtract))
            er = z[6]
            lr, li = zt[:, 1, 0, :], zt[:, 1, 1, :]
            link(V.tensor_tensor(w, qa, c, ALU.mult))
            link(V.tensor_tensor(z[12], qb, s, ALU.mult))
            link(V.tensor_tensor(w, w, z[12], ALU.subtract))
            link(V.tensor_tensor(lr, w, er, ALU.mult))
            link(V.tensor_tensor(w, qa, s, ALU.mult))
            link(V.tensor_tensor(z[12], qb, c, ALU.mult))
            link(V.tensor_tensor(w, w, z[12], ALU.add))
            link(V.tensor_tensor(li, w, er, ALU.mult))
            link(V.memset(zt[:, 0, 0, :], 1.0))
            link(V.memset(zt[:, 0, 1, :], 0.0))

            def power(k0, k1, by):
                cnt_ = k1 - k0 + 1
                A_r, A_i = zt[:, k0:k1 + 1, 0, :], zt[:, k0:k1 + 1, 1, :]
                b_r = zt[:, by:by + 1, 0, :].to_broadcast([P, cnt_, ST])
                b_i = zt[:, by:by + 1, 1, :].to_broadcast([P, cnt_, ST])
                x1, x2, x3, x4 = (t[:, 0:cnt_, :] for t in (t1, t2, t3, t4))
                V.tensor_tensor(x1, A_r, b_r, ALU.mult)
                V.tensor_tensor(x2, A_i, b_i, ALU.mult)
                V.tensor_tensor(x3, A_r, b_i, ALU.mult)
                link(V.tensor_tensor(x4, A_i, b_r, ALU.mult))
                V.tensor_tensor(zt[:, k0 + by:k1 + by + 1, 0, :], x1, x2, ALU.subtract)
                link(V.tensor_tensor(zt[:, k0 + by:k1 + by + 1, 1, :], x3, x4, ALU.add))
            power(1, 1, 1)
            power(1, 2, 2)
            l1, d1, d2 = z[12], z[1], z[2]
            link(V.tensor_scalar(l1, lr, 1.0, None, ALU.subtract))
            link(V.tensor_tensor(d1, are, are, ALU.mult))
            link(V.tensor_tensor(d2, aim, aim, ALU.mult))
            link(V.tensor_tensor(d1, d1, d2, ALU.add))
            link(V.reciprocal(d1, d1))
            link(V.tensor_tensor(z[3], l1, are, ALU.mult))
            link(V.tensor_tensor(z[7], li, aim, ALU.mult))
            link(V.tensor_tensor(z[3], z[3], z[7], ALU.add))
            link(V.tensor_tensor(zt[:, NK, 0, :], z[3], d1, ALU.mult))
            link(V.tensor_tensor(z[3], li, are, ALU.mult))
            link(V.tensor_tensor(z[7], l1, aim, ALU.mult))
            link(V.tensor_tensor(z[3], z[3], z[7], ALU.subtract))
            V.tensor_tensor(zt[:, NK, 1, :], z[3], d1, ALU.mult).then_inc(tab_ready, 1)
            dve.wait_ge(inputs_in, 7 * 16)
            for b in range(2):
                last = V.tensor_scalar(l8m[:, :, b, :], zt[:, CHUNK, :, :], con[:, C_MZ + b:C_MZ + b + 1],
                                       None, ALU.mult)
            last.then_inc(l8_masked, 1)
            dve.wait_ge(l8_done, 1)
            for k in range(2):
                link(V.tensor_copy(t1[:, 0:2, :].rearrange("p a c -> p (a c)"), ps[:, k, 0:P]))
                v = t1[:, 0:2, :].rearrange("p a (c b) -> p (a c) b", b=2)
                link(V.tensor_tensor(L8[:, k, :], v[:, :, 0], v[:, :, 1], ALU.add))
            link(V.tensor_scalar(L8[:, 2, :], L8[:, 1, :], -1.0, None, ALU.mult))

            for b in range(2):
                last = V.memset(ps[:, 6 + b, :], 0.0)
            last.then_inc(mod_bank_zero, 1)

            base = steps[0]
            PER = 11
            with dve.Fori(0, MB) as i2:
              for h in range(2):
                i = i2 * 2 + h
                XL, BC = XLs[h], BCs[h]
                k = 0

                def step(ins):
                    nonlocal k
                    k += 1
                    ins.then_inc(dve_step, 1)
                    dve.wait_ge(dve_step, base + i * PER + k)

                def two(o1, o2, ar, ai, br, bi, x, neg=False):
                    V.tensor_tensor(x[0], ar, br, ALU.mult)
                    V.tensor_tensor(x[1], ai, bi, ALU.mult)
                    V.tensor_tensor(x[2], ar, bi, ALU.mult)
                    step(V.tensor_tensor(x[3], ai, br, ALU.mult))
                    V.tensor_tensor(o1, x[0], x[1], ALU.subtract)
                    return V.tensor_tensor(o2, x[2], x[3], ALU.add)

                dve.wait_ge(xl_in[h], i2 * 48 + 48)
                wr, wi = XL[:, :, NK, 0, :], XL[:, :, NK, 1, :]
                x = [t[:, 0:2, :] for t in (t1, t2, t3, t4)]
                step(two(Bb[:, :, 0, :], Bb[:, :, 1, :], wr, wi, BC[:, 0, :, 0, :], BC[:, 0, :, 1, :], x))
                for d in range(2):
                    br = Bb[:, d, 0:1, :].to_broadcast([P, CHUNK, ST])
                    bi = Bb[:, d, 1:2, :].to_broadcast([P, CHUNK, ST])
                    x = [t[:, 0:CHUNK, :] for t in (t1, t2, t3, t4)]
                    ins = two(BP[:, d, 0], BP[:, d, 1], XL[:, d, 0:CHUNK, 0, :], XL[:, d, 0:CHUNK, 1, :], br, bi, x)
                    if d == 0:
                        step(ins)
                ins.then_inc(bp_made, 1)
                dve.wait_ge(bp_made, i + 1)
                for d in range(2):
                    cr = BC[:, 1, d, 0:1, :].to_broadcast([P, NK, ST])
                    ci = BC[:, 1, d, 1:2, :].to_broadcast([P, NK, ST])
                    x = [t[:] for t in (t1, t2, t3, t4)]
                    step(two(CP[:, d, 0], CP[:, d, 1], XL[:, d, 0:NK, 0, :], XL[:, d, 0:NK, 1, :], cr, ci, x))
                V.tensor_scalar(CP[:, :, 1].rearrange("p a k s -> p a (k s)"),
                                CP[:, :, 1].rearrange("p a k s -> p a (k s)"), -1.0, None,
                                ALU.mult).then_inc(cp_made, 1)
                dve.wait_ge(kb_free, i * 16 + 16)
                dve.wait_ge(taps_done, i + 1)
                blk = con[:, C_BLK:C_BLK + P].unsqueeze(1).to_broadcast([P, CHUNK, P])
                for d in range(2):
                    ins = V.tensor_tensor(KB[:, CHUNK * d:CHUNK * d + CHUNK, :],
                                          ps[:, 2 + d, :].rearrange("p (k c) -> p k c", k=CHUNK), blk, ALU.mult)
                step(ins)
                step(V.tensor_tensor(KB[:, 0, :], KB[:, 0, :], KB[:, CHUNK, :], ALU.add))
                V.tensor_copy(KB[:, CHUNK, :], KB[:, 2 * CHUNK - 1, :]).then_inc(kb_made, 1)
                for j in range(RING):
                    n = i * RING + j
                    dve.wait_ge(mod_cols_done, n + 1)
                    V.tensor_tensor(modf[:, bass.ds(n * 4, 4), :],
                                    ps[:, 4, 8 * j:8 * j + 8].rearrange("p (a c) -> p a c", c=2),
                                    bmodf[:, bass.ds(n * 4, 4)].unsqueeze(2).to_broadcast([P, 4, 2]),
                                    ALU.add).then_inc(mod_cols_taken, 1)
                assert k == PER, k
            steps[0] = base + PER * 2 * MB

            dve.wait_ge(xl_in[0], 48 * (MB + 1))
            for s_ in (bp_free, cp_free, kb_free):
                dve.wait_ge(s_, 16 * (2 * MB + 1))
            dve.wait_ge(mod_cols_taken, ADA)
            for l in range(DEPTH):
                for n_, o in ((0, 8), (1, 32)):
                    link(V.tensor_scalar(nsc[:, 2 * l + n_], modv[:, l, o:o + 8, :], 1.0, None, ALU.add))
                    link(V.tensor_tensor(nsc[:, 2 * l + n_], nsc[:, 2 * l + n_],
                                         gains[:, 2 * l + n_, :].unsqueeze(2).to_broadcast([P, KD, 2]), ALU.mult))

            def norm(l, n_):
                lo = CTX if (l, n_) == (1, 1) else 0
                V.tensor_tensor(aT[:, :, lo:NT], hT[:, :, lo:NT], hT[:, :, lo:NT], ALU.mult).then_inc(sq_ready, 1)
                taken(dve, ("ss", l, n_))
                link(V.reciprocal(rms[:, lo:NT], rms[:, lo:NT]))
                link(V.tensor_tensor(aT[:, :, lo:NT], hT[:, :, lo:NT],
                                     rms[:, lo:NT].unsqueeze(1).to_broadcast([P, KD, NT - lo]), ALU.mult))
                sh = 24 * n_
                for kk in range(KD):
                    for s_ in range(lo // CTX, 2):
                        v = aT[:, kk, 256 * s_:256 * s_ + 256]
                        last = V.tensor_scalar(v, v, nsc[:, 2 * l + n_, kk, s_:s_ + 1],
                                               modv[:, l, sh + kk, s_:s_ + 1], ALU.mult, ALU.add)
                last.then_inc(a_ready, 1)

            def residual(key, l, m, gate, lo):
                bank, free = arrived(dve, key)
                for s_ in range(lo // CTX, 2):
                    v = hT[:, m, 256 * s_:256 * s_ + 256]
                    last = V.scalar_tensor_tensor(v, bank[:, 256 * s_ - lo:256 * s_ - lo + 256],
                                                  modv[:, l, gate + m, s_:s_ + 1], v, ALU.mult, ALU.add)
                last.then_inc(free, 1)

            scans = [0]
            for l in range(DEPTH):
                t0 = CTX * l
                n_ = NT - t0
                norm(l, 0)
                if l == 0:
                    link(V.memset(H[:, 0], 0.0))
                for m in range(4):
                    for g in range(4):
                        bank, free = arrived(dve, ("E", l, m, g))
                        ev = bank[:, 0:4 * NCH].rearrange("p (d r c) -> p d c r", d=2, r=2)
                        col = m * 8 + g
                        V.tensor_copy(H[:, 1:NCH + 1, :, col], ev[:, 0])
                        V.tensor_copy(H[:, 1:NCH + 1, :, col + 4].rearrange("p (s c) r -> p s c r", s=2),
                                      ev[:, 1].rearrange("p (s c) r -> p s c r", s=2)[:, :, ::-1, :]).then_inc(free, 1)
                taken(dve, ("E", l, 3, 3))
                l8r = L8[:, 0:1, 32 * l:32 * l + 32].to_broadcast([P, 2, 32])
                l8x = L8[:, 1:3, 32 * l:32 * l + 32]
                UN = 8
                sb0 = scans[0]
                with dve.Fori(0, NCH // UN) as i:
                    for u in range(UN):
                        now = H[:, bass.ds(i * UN + u, 1), :, :].rearrange("p o r c -> p (o r) c")
                        nxt = H[:, bass.ds(i * UN + (u + 1), 1), :, :].rearrange("p o r c -> p (o r) c")
                        if u:
                            dve.wait_ge(scan_step, sb0 + i * (4 * UN) + 4 * u)
                        V.tensor_tensor(sc1[:], now, l8r, ALU.mult).then_inc(scan_step, 1)
                        V.tensor_tensor(sc2[:, ::-1, :], now, l8x, ALU.mult).then_inc(scan_step, 1)
                        dve.wait_ge(scan_step, sb0 + i * (4 * UN) + 4 * u + 1)
                        V.tensor_tensor(sc1[:], sc1[:], nxt, ALU.add).then_inc(scan_step, 1)
                        dve.wait_ge(scan_step, sb0 + i * (4 * UN) + 4 * u + 3)
                        V.tensor_tensor(nxt, sc1[:], sc2[:], ALU.add).then_inc(scan_step, 1)
                    dve.wait_ge(scan_step, sb0 + i * (4 * UN) + 4 * UN)
                scans[0] = sb0 + 4 * NCH
                for m in range(8):
                    taken(dve, ("ga", l, m))
                    bank, free = arrived(dve, ("ya", l, m))
                    V.tensor_tensor(G[:, m, t0:NT], G[:, m, t0:NT], bank[:, 0:n_], ALU.mult).then_inc(free, 1)
                for m in range(4):
                    if m >= 2:
                        dve.wait_ge(ys_ready, 4 * l + m - 1)
                    bank, free = arrived(dve, ("Y", l, m))
                    V.scalar_tensor_tensor(ypre[:, m % 2, t0:NT], uT[:, m, t0:NT], dskip[:, l, m:m + 1],
                                           bank[:, 0:n_], ALU.mult, ALU.add).then_inc(free, 1)
                for m in range(8):
                    taken(dve, ("glub", l, m))
                    taken(dve, ("gb", l, m))
                    bank, free = arrived(dve, ("glua", l, m))
                    V.tensor_tensor(aT[:, m, t0:NT], aT[:, m, t0:NT], bank[:, 0:n_], ALU.mult).then_inc(free, 1)
                    taken(dve, ("glua", l, m))
                    link(V.tensor_tensor(G2[:, m, t0:NT], G2[:, m, t0:NT], aT[:, m, t0:NT], ALU.mult))
                    V.tensor_tensor(G[:, m, t0:NT], G[:, m, t0:NT], G2[:, m, t0:NT], ALU.add).then_inc(mix_ready, 1)
                for m in range(8):
                    residual(("out", l, m), l, m, 16, t0)
                taken(dve, ("out", l, 7))
                norm(l, 1)
                if l == 0:
                    for m in range(FB):
                        taken(dve, ("gate", l, m))
                        bank, free = arrived(dve, ("up", l, m))
                        V.tensor_tensor(hid[:, m, :], sg[:, m % 2, :], bank[:, 0:NT], ALU.mult).then_inc(free, 1)
                    for m in range(8):
                        residual(("down", l, m), l, m, 40, 0)
                    taken(dve, ("down", l, 7))

            dve.wait_ge(logits_done, 1)
            link(V.tensor_tensor(lg[:], ps[:, 7, 0:16].rearrange("p (a e) -> p a e", a=2),
                                 brt[:].unsqueeze(1).to_broadcast([P, 2, NE]), ALU.add))
            for t in range(2):
                link(V.max(mx[:, t, :], lg[:, t, :]))
                link(V.max_index(mi[:, t, :], mx[:, t, :], lg[:, t, :]))
            link(V.tensor_copy(mif[:], mi[:]))
            V.tensor_tensor(wt[:, :, 0:1], mx[:, :, 1:2], mx[:, :, 0:1], ALU.subtract).then_inc(top_ready, 1)
            iota = con[:, C_IOTA:C_IOTA + 256]
            for t in range(2):
                for j in range(2):
                    link(V.tensor_scalar(oh[:, t, j, :], iota[:, 0:NE], mif[:, t, j:j + 1], None, ALU.is_equal))
            V.tensor_tensor(sel[:], oh[:, :, 0, :], oh[:, :, 1, :], ALU.add).then_inc(sel_ready, 1)
            dve.wait_ge(weights_exp, 1)
            link(V.tensor_scalar(wt[:, :, 2:3], wt[:, :, 1:2], 1.0, None, ALU.add))
            link(V.reciprocal(wt[:, :, 2:3], wt[:, :, 2:3]))
            link(V.tensor_tensor(wt[:, :, 3:4], wt[:, :, 1:2], wt[:, :, 2:3], ALU.mult))
            for t in range(2):
                link(V.tensor_scalar(comb[:, t, :], oh[:, t, 0, :], wt[:, t, 2:3], None, ALU.mult))
                link(V.scalar_tensor_tensor(comb[:, t, :], oh[:, t, 1, :], wt[:, t, 3:4], comb[:, t, :],
                                            ALU.mult, ALU.add))
            dve.wait_ge(rank_done, 1)
            link(V.tensor_scalar(rank[:], sel[:], -4096.0, 4096.0, ALU.mult, ALU.add))
            link(V.tensor_tensor(rank[:], rank[:], ps[:, 7, 16:32].rearrange("p (a e) -> p a e", a=2), ALU.add))
            link(V.reduce_max(cnt[:], ps[:, 7, 32:40], AX.X))
            V.tensor_copy(cnti[:], cnt[:]).then_inc(count_ready, 1)

            def experts(pas):
                base_ = steps[0]
                with dve.Fori(0, NE) as e:
                    x = e + NE * pas
                    for t in range(2):
                        V.tensor_scalar(S[:, t, :], iota[:, P * pas:P * pas + P], rank[:, t, bass.ds(e, 1)],
                                        None, ALU.is_equal)
                        last = V.tensor_scalar(SW[:, t, :], iota[:, P * pas:P * pas + P],
                                               rank[:, t, bass.ds(e, 1)], comb[:, t, bass.ds(e, 1)],
                                               ALU.is_equal, ALU.mult)
                    last.then_inc(onehot_ready, 1)
                    for c in range(FCH):
                        dve.wait_ge(gate_taken, x * FCH + c + 1)
                        dve.wait_ge(gateup_done, x * 2 * FCH + 2 * c + 2)
                        if c >= 2:
                            dve.wait_ge(misc_done, x * MISC + 3 + c - 1)
                        V.tensor_tensor(hd[:, c % 2, :], gs[:, c % 2, :], ps[:, 2 * (c % 2) + 1, :],
                                        ALU.mult).then_inc(hid_ready, 1)
                    for j in range(4):
                        u = 3 + FCH + j
                        dve.wait_ge(misc_done, x * MISC + u + 1)
                        for i_ in range(2):
                            v = hT[:, 2 * j + i_, CTX:NT]
                            last = V.scalar_tensor_tensor(v, ps[:, 6 + u % 2, 256 * i_:256 * i_ + 256],
                                                          modv[:, 1, 40 + 2 * j + i_, 1:2], v, ALU.mult, ALU.add)
                        last.then_inc(misc_taken[u % 2], 1)
                    dve.wait_ge(misc_taken[(3 + FCH + 3) % 2], x * (MISC // 2) + MISC // 2)
            experts(0)
            most = dve.value_load(cnti[0:1, 0:1], min_val=0, max_val=SEQ)
            with dve.If(most > P):
                experts(1)
            V.tensor_tensor(aT[:, :, CTX:NT], hT[:, :, CTX:NT], hT[:, :, CTX:NT], ALU.mult).then_inc(sq_ready, 1)
            dve.wait_ge(root_ready, 1)
            link(V.reciprocal(rms[:, 0:SEQ], rms[:, 0:SEQ]))
            link(V.tensor_tensor(aT[:, :, CTX:NT], hT[:, :, CTX:NT],
                                 rms[:, 0:SEQ].unsqueeze(1).to_broadcast([P, KD, SEQ]), ALU.mult))
            V.tensor_tensor(aT[:, :, CTX:NT], aT[:, :, CTX:NT],
                            gains[:, 4, :].unsqueeze(2).to_broadcast([P, KD, SEQ]), ALU.mult).then_inc(out_ready, 1)

        @block.tensor
        def _(pe):
            mm = nc.tensor.matmul
            pe.wait_ge(inputs_in, 7 * 16)
            pe.wait_ge(l8_masked, 1)
            for k in range(2):
                last = nc.tensor.transpose(ps[:, k, 0:P], l8m[:, k].rearrange("p b s -> p (b s)"), ident)
            last.then_inc(l8_done, 1)
            pe.wait_ge(silu_c_ready, 1)
            pe.wait_ge(mod_bank_zero, 1)
            with pe.Fori(0, 2 * MB) as i:
                def turn(j):
                    pe.wait_ge(mod_rows_taken, i * RING + j + 1)
                    for q in range(4):
                        last = mm(ps[:, 4, 8 * j + 2 * q:8 * j + 2 * q + 2], mrow[:, j % 2, P * q:P * q + P],
                                  con[:, C_SEL:C_SEL + 2], start=True, stop=True)
                    last.then_inc(mod_cols_done, 1)
                for j in range(RING):
                    pe.wait_ge(landed[j], i * 16 + 16)
                    if j >= 2:
                        pe.wait_ge(mod_rows_taken, i * RING + j - 1)
                    wv = ring[j][:].rearrange("p (k c) -> p k c", k=KD)
                    for k in range(KD):
                        g = 32 * (k % 4)
                        last = mm(ps[g:g + 2, 6 + j % 2, :], silu_c[:, k, :], wv[:, k, :],
                                  start=(k < 4), stop=(k >= 4), skip_group_check=True)
                    last.then_inc(mod_rows_done, 1)
                    if j >= 1:
                        turn(j - 1)
                turn(RING - 1)
                pe.wait_ge(cp_masked, i * 2 + 2)
                pe.wait_ge(bp_masked, i * 2 + 2)
                cpv = CPm[:].rearrange("p a b k c s -> p (a b k) (c s)")
                bpv = BPm[:].rearrange("p a b k c s -> p (a b) k (c s)")
                for g in range(NK + 1):
                    if g >= 2:
                        pe.wait_ge(tr_taken, i * (NK + 1) + g - 1)
                    for j in range(4):
                        n = 4 * g + j
                        src = cpv[:, n, :] if n < 4 * NK else bpv[:, n - 4 * NK, 0, :]
                        last = nc.tensor.transpose(ps[:, g % 2, P * j:P * j + P], src, ident)
                    last.then_inc(tr_done, 1)
                pe.wait_ge(tr_taken, i * (NK + 1) + (NK + 1))
                for d in range(2):
                    for r in range(2):
                        o = (d * 2 + r) * NK
                        last = mm(ps[:, 2 + d, :], CTr[:, 4 * NK + d * 2 + r, :],
                                  CTr[:, o:o + CHUNK, :].rearrange("p a c -> p (a c)"), start=(r == 0), stop=(r == 1))
                last.then_inc(taps_done, 1)
                pe.wait_ge(kb_made, i + 1)
                pe.wait_ge(mod_cols_taken, i * RING + RING)

            def slot(key):
                n = stream_at[key]
                pe.wait_ge(landed[n % RING], 16 * (n // RING + 1))
                return ring[n % RING]

            def product(key, pairs, cols=NT, inc=None):
                bank = bank_for(pe, key)
                for k, (w, x) in enumerate(pairs):
                    last = mm(bank[:, 0:cols], w, x, start=(k == 0), stop=(k == len(pairs) - 1))
                last.then_inc(place(key)[1], 1)

            def sums(l, n):
                lo = CTX if (l, n) == (1, 1) else 0
                pe.wait_ge(sq_ready, 2 * l + n + 1)
                bank = bank_for(pe, ("ss", l, n))
                for k in range(KD):
                    last = mm(bank[:, lo:NT], ones, aT[:, k, lo:NT], start=(k == 0), stop=(k == KD - 1))
                last.then_inc(dense_done, 1)

            for l in range(DEPTH):
                t0 = CTX * l
                n_ = NT - t0
                sums(l, 0)
                pe.wait_ge(a_ready, 2 * l + 1)
                for name, tile, lo in (("u", 1, 0), ("f", 0, t0)):
                    w = slot(("w_in", l, tile))[:].rearrange("p (k c) -> p k c", k=KD)
                    for m in range(4):
                        product((name, l, m), [(w[:, k, P * m:P * m + P], aT[:, k, lo:NT]) for k in range(KD)],
                                NT - lo)
                for m in range(4):
                    taken(pe, ("u", l, m))
                    w = slot(("bp", l, m // 2))[:].rearrange("p (m d r k c) -> p m d r k c", m=2, d=2, r=2,
                                                             k=CHUNK)[:, m % 2]
                    uc = uT[:, m, :].rearrange("p (c j) -> p c j", j=CHUNK)
                    for g in range(4):
                        bank = bank_for(pe, ("E", l, m, g))
                        rows = slice(32 * g, 32 * g + 32)
                        for d in range(2):
                            for r in range(2):
                                o = (d * 2 + r) * NCH
                                for j in range(CHUNK):
                                    k = j if d else CHUNK - 1 - j
                                    last = mm(bank[:, o:o + NCH], w[rows, d, r, k, :], uc[rows, :, j],
                                              start=(j == 0), stop=(j == CHUNK - 1))
                        last.then_inc(side_done, 1)
                for m in range(4):
                    taken(pe, ("f", l, m))
                    for t in range(2 * l, 4):
                        product(("dft1", l, m, t), [(uF[:, m, P * t:P * t + P], con[:, C_CS:C_CS + 256])], 256)
                for m in range(4):
                    for s in range(l, 2):
                        pairs = []
                        for k in range(2):
                            t = 2 * s + k
                            taken(pe, ("dft1", l, m, t))
                            pairs += [(Q[:, t, m, 0:P], con[:, C_CN + 256 * k:C_CN + 256 * k + 256]),
                                      (Q[:, t, m, P:2 * P], con[:, C_SN + 256 * k:C_SN + 256 * k + 256])]
                        product(("dft2", l, m, s), pairs, 256)
                for name, tile in (("ga", 2), ("gb", 4)):
                    for h in range(2):
                        w = slot(("w_in", l, tile + h))[:].rearrange("p (k c) -> p k c", k=KD)
                        for m in range(4):
                            product((name, l, 4 * h + m),
                                    [(w[:, k, P * m:P * m + P], aT[:, k, t0:NT]) for k in range(KD)], n_)
                w = slot(("w_four", l, 0))[:].rearrange("p (k c) -> p k c", k=MB)
                for m in range(4):
                    taken(pe, ("dft2", l, m, 1))
                for m in range(8):
                    product(("ya", l, m), [(w[:, k, P * m:P * m + P], uF[:, k, t0:NT]) for k in range(MB)], n_)
                pe.wait_ge(scan_step, 4 * NCH * (l + 1))
                c0 = t0 // CHUNK
                for m in range(4):
                    bank = bank_for(pe, ("Y", l, m))
                    out_c = bank[:, 0:n_].rearrange("p (c j) -> p c j", j=CHUNK)
                    uc = uT[:, m, t0:NT].rearrange("p (c j) -> p c j", j=CHUNK)
                    tile = slot(("ck", l, m))
                    w = tile[:, CPW:CKW].rearrange("p (k c) -> p k c", k=2 * CHUNK - 1)
                    for k in range(CHUNK):
                        mm(out_c[:, :, k:CHUNK], w[:, k, :], uc[:, :, 0:CHUNK - k], start=(k == 0), stop=(k == 0), skip_group_check=True)
                        if k:
                            last = mm(out_c[:, :, 0:CHUNK - k], w[:, CHUNK + k % (CHUNK - 1), :], uc[:, :, k:CHUNK],
                                      start=False, stop=False, skip_group_check=True)
                    w = tile[:, 0:CPW].rearrange("p (d r k c) -> p d r k c", d=2, r=2, k=CHUNK)
                    for g in range(4):
                        rows = slice(32 * g, 32 * g + 32)
                        for r in range(2):
                            for j in range(CHUNK):
                                col = m * 8 + g
                                mm(out_c[rows, :, j], w[:, 0, r, j, rows], H[:, c0:NCH, r, col],
                                   start=False, stop=False, skip_group_check=True)
                                hv = H[:, 0:NCH, r, col + 4].rearrange("p (s c) -> p s c", s=2)[:, l:2, ::-1]
                                last = mm(out_c[rows, :, j].rearrange("p (s c) -> p s c", s=2 - l),
                                          w[:, 1, r, CHUNK - 1 - j, rows], hv,
                                          start=False, stop=(g == 3 and r == 1 and j == CHUNK - 1), skip_group_check=True)
                    last.then_inc(side_done, 1)
                for name in ("glub", "glua"):
                    w = slot(("w_" + name[:3] + "_" + name[3], l, 0))[:].rearrange("p (k c) -> p k c", k=MB)
                    pe.wait_ge(ys_ready, 4 * l + 4)
                    for m in range(8):
                        product((name, l, m), [(w[:, k, P * m:P * m + P], ysT[:, k, t0:NT]) for k in range(MB)], n_)
                pe.wait_ge(mix_ready, 8 * l + 8)
                for h in range(2):
                    w = slot(("w_out", l, h))[:].rearrange("p (k c) -> p k c", k=KD)
                    for m in range(4):
                        product(("out", l, 4 * h + m),
                                [(w[:, k, P * m:P * m + P], G[:, k, t0:NT]) for k in range(KD)], n_)
                sums(l, 1)
                pe.wait_ge(a_ready, 2 * l + 2)
                if l == 0:
                    for t in range(FB // 2):
                        w = slot(("ffn_gu", l, t))[:].rearrange("p (u k c) -> p u k c", u=2, k=KD)
                        for m in range(2):
                            for u, name in enumerate(("gate", "up")):
                                product((name, l, 2 * t + m),
                                        [(w[:, u, k, P * m:P * m + P], aT[:, k, :]) for k in range(KD)])
                    taken(pe, ("up", l, FB - 1))
                    for t in range(4):
                        ws = [slot(("ffn_down", l, 2 * t + h))[:, 0:11 * 256].rearrange("p (k c) -> p k c", k=11)
                              for h in range(2)]
                        for m in range(2):
                            product(("down", l, 2 * t + m),
                                    [(ws[k // 11][:, k % 11, P * m:P * m + P], hid[:, k, :]) for k in range(FB)])

            for t in range(2):
                for k in range(KD):
                    last = mm(ps[:, 7, NE * t:NE * t + NE], aT[:, k, CTX + P * t:CTX + P * t + P], wrt[:, k, :],
                              start=(k == 0), stop=(k == KD - 1))
            last.then_inc(logits_done, 1)
            for g in range(4):
                for j in range(4):
                    k = 4 * (g % 2) + j
                    last = nc.tensor.transpose(ps[:, g, P * j:P * j + P],
                                               aT[:, k, CTX + P * (g // 2):CTX + P * (g // 2) + P], ident)
                last.then_inc(ftok_done, 1)
            pe.wait_ge(sel_ready, 1)
            tri = con[:, C_TRI:C_TRI + P]
            mm(ps[:, 7, 16:24], tri, sel[:, 0, :], start=True, stop=True)
            mm(ps[:, 7, 24:32], ones, sel[:, 0, :], start=True, stop=False)
            mm(ps[:, 7, 24:32], tri, sel[:, 1, :], start=False, stop=True)
            mm(ps[:, 7, 32:40], ones, sel[:, 0, :], start=True, stop=False)
            mm(ps[:, 7, 32:40], ones, sel[:, 1, :], start=False, stop=True).then_inc(rank_done, 1)
            pe.wait_ge(ftok_ready, 4)
            pe.wait_ge(count_ready, 1)

            def experts(pas):
                with pe.Fori(0, NE) as e:
                    x = e + NE * pas

                    def mslot(kind, c):
                        t = moe_at[(kind, c)]
                        pe.wait_ge(mlanded[t % MRING], x * 48 + 16 * (t // MRING + 1))
                        return mring[t % MRING]

                    def misc(u):
                        if u >= 2:
                            pe.wait_ge(misc_taken[u % 2], x * (MISC // 2) + u // 2)
                        return ps[:, 6 + u % 2, :]
                    pe.wait_ge(onehot_ready, x + 1)
                    for g in range(2):
                        bank = misc(g)
                        for k in range(4):
                            for t in range(2):
                                o = P * (4 * g + k)
                                last = mm(bank[:, P * k:P * k + P], ftok[:, t, o:o + P], S[:, t, :],
                                          start=(t == 0), stop=(t == 1))
                        last.then_inc(misc_done, 1)
                    bank = misc(2)
                    for t in range(2):
                        last = nc.tensor.transpose(bank[:, P * t:P * t + P], SW[:, t, :], ident)
                    last.then_inc(misc_done, 1)
                    for g in range(2):
                        pe.wait_ge(misc_taken[g], x * (MISC // 2) + 1)

                    def down(c):
                        bank = misc(3 + c)
                        pe.wait_ge(hid_ready, x * FCH + c + 1)
                        for j in range(4):
                            last = nc.tensor.transpose(bank[:, P * j:P * j + P], hd[:, c % 2, P * j:P * j + P], ident)
                        last.then_inc(misc_done, 1)
                        w = mslot("down", c)[:].rearrange("p (k c) -> p k c", k=4)
                        pe.wait_ge(misc_taken[(3 + c) % 2], x * (MISC // 2) + (3 + c) // 2 + 1)
                        for h in range(2):
                            for j in range(4):
                                last = mm(ps[:, 4 + h, :], hTc[:, c % 2, j, :], w[:, j, 512 * h:512 * h + 512],
                                          start=(c == 0 and j == 0), stop=(c == FCH - 1 and j == 3))
                        last.then_inc(down_done, 1)
                    for c in range(FCH):
                        for u in range(2):
                            w = mslot(("gate", "up")[u], c)[:].rearrange("p (k c) -> p k c", k=KD)
                            if c >= 2:
                                pe.wait_ge(hid_ready, x * FCH + c - 1)
                            for k in range(KD):
                                last = mm(ps[:, 2 * (c % 2) + u, :], XG[:, k, :], w[:, k, :],
                                          start=(k == 0), stop=(k == KD - 1))
                            last.then_inc(gateup_done, 1)
                        if c >= 1:
                            down(c - 1)
                    down(FCH - 1)
                    pe.wait_ge(ye_ready, x * 2 + 2)
                    for j in range(4):
                        bank = misc(3 + FCH + j)
                        for i_ in range(2):
                            m = 2 * j + i_
                            last = mm(bank[:, 256 * i_:256 * i_ + 256], ye[:, P * m:P * m + P], SWT[:],
                                      start=True, stop=True)
                        last.then_inc(misc_done, 1)
                    for g in range(2):
                        pe.wait_ge(misc_taken[g], x * (MISC // 2) + MISC // 2)
            experts(0)
            most = pe.value_load(cnti[0:1, 0:1], min_val=0, max_val=SEQ)
            with pe.If(most > P):
                experts(1)
            pe.wait_ge(sq_ready, 2 * DEPTH + 1)
            for k in range(KD):
                last = mm(ps[:, 0, 0:SEQ], ones, aT[:, k, CTX:NT], start=(k == 0), stop=(k == KD - 1))
            last.then_inc(fin_done, 1)


def layout(x, c, ctx, c_ctx, w_mod, b_mod, norm1_g, norm2_g, w_in, w_four, ssm_a_re, ssm_a_im, ssm_log_dt,
           ssm_b_re, ssm_b_im, ssm_c_re, ssm_c_im, ssm_d, w_glu_a, w_glu_b, w_out, ffn_w_gate, ffn_w_up,
           ffn_w_down, moe_w_router, moe_b_router, moe_w_gate, moe_w_up, moe_w_down, final_g):
    def cut(w, rows, cols):
        lead = w.shape[:-2]
        k, n = w.shape[-2:]
        w = w.reshape(*lead, k // P, P, n // cols, cols)
        nl = len(lead)
        w = w.transpose(*range(nl), nl + 2, nl + 1, nl, nl + 3)
        return w.reshape(*lead, n // cols, P, (k // P) * cols)

    def vec(v):
        v = v.reshape(*v.shape[:-1], v.shape[-1] // P, P)
        return np.moveaxis(v, -1, 0)

    def rows(v):
        v = v.reshape(DEPTH, 2, MB, 8, *v.shape[3:])
        return v.swapaxes(1, 2)

    r = {"con": constants(), "pos": positions()}
    tok = np.concatenate([ctx[0], x[0]], axis=0)
    r["xT"] = tok.T.reshape(KD, P, NT).transpose(1, 0, 2)
    r["cT"] = np.stack([vec(c_ctx), vec(c[0])], axis=-1)
    r["w_mod"] = cut(w_mod, D, 512).reshape(ADA_TILES, P, SLOT)
    r["bmod"] = vec(b_mod)
    r["gains"] = vec(np.stack([norm1_g[0], norm2_g[0], norm1_g[1], norm2_g[1], final_g]))
    r["w_in"] = cut(w_in, D, 512)
    r["w_out"] = cut(w_out, D, 512)
    for n, w in (("w_four", w_four), ("w_glu_a", w_glu_a), ("w_glu_b", w_glu_b)):
        r[n] = cut(w, WF, D)[:, 0]
    r["lam"] = np.stack([rows(ssm_a_re), rows(ssm_a_im)], axis=-2).reshape(P, 2, ST)
    r["ldt"] = rows(ssm_log_dt).reshape(P, 1)
    b = np.stack([rows(ssm_b_re), rows(ssm_b_im)], axis=3).transpose(0, 1, 4, 6, 2, 3, 5)
    cc = np.stack([rows(ssm_c_re), rows(ssm_c_im)], axis=3).transpose(0, 1, 4, 5, 2, 3, 6)
    r["bc"] = np.stack([b, cc], axis=4).reshape(2 * MB, P, 2 * 2 * 2 * ST)
    r["dskip"] = vec(ssm_d)
    g = cut(ffn_w_gate[0], D, 256)
    u = cut(ffn_w_up[0], D, 256)
    r["ffn_gu"] = np.concatenate([g, u], axis=-1)
    dn = ffn_w_down[0].reshape(2, FB // 2, P, 4, 256).transpose(3, 0, 2, 1, 4)
    r["ffn_down"] = dn.reshape(8, P, (FB // 2) * 256)
    r["wrt"] = moe_w_router[0].reshape(KD, P, NE).transpose(1, 0, 2)
    r["brt"] = np.broadcast_to(moe_b_router[0], (P, NE))
    r["moe_gate"] = cut(moe_w_gate[0], D, 512).reshape(NE * FCH, P, SLOT)
    r["moe_up"] = cut(moe_w_up[0], D, 512).reshape(NE * FCH, P, SLOT)
    r["moe_down"] = moe_w_down[0].reshape(NE, FCH, 4, P, D).transpose(0, 1, 3, 2, 4).reshape(NE * FCH, P, SLOT)
    return {k: np.ascontiguousarray(v) for k, v in r.items()}


def declare(nc, arrays):
    a = {k: nc.dram_tensor("in_" + k, v.shape, F32, kind="ExternalInput").ap() for k, v in arrays.items()}
    out = nc.dram_tensor("out", (P, KD, SEQ), F32, kind="ExternalOutput").ap()
    tab = nc.dram_tensor("tab", (P, TAB), F32, kind="Internal").ap()
    bps = nc.dram_tensor("bps", (2 * MB, P, 8 * CHUNK * ST), F32, kind="Internal").ap()
    cks = nc.dram_tensor("cks", (2 * MB, P, CKW), F32, kind="Internal").ap()
    program(nc, a, out, tab, bps, cks)


def kernel(**inputs):
    import concourse.bacc as bacc
    from concourse.bass_utils import run_bass_kernel_spmd

    arrays = layout(**{k: np.asarray(v) for k, v in inputs.items()})
    nc = bacc.Bacc("TRN2", target_bir_lowering=False, num_devices=1)
    declare(nc, arrays)
    r = run_bass_kernel_spmd(nc, [{"in_" + k: v for k, v in arrays.items()}], core_ids=[0])
    y = r.results[0]["out"]
    return np.ascontiguousarray(y.transpose(1, 0, 2).reshape(D, SEQ).T)[None]
```

```python
from contextlib import ExitStack

import numpy as np
import concourse.bass as bass
from concourse import mybir

F32 = mybir.dt.float32
F32R = mybir.dt.float32r
I32 = mybir.dt.int32
U32 = mybir.dt.uint32
ALU = mybir.AluOpType
ACT = mybir.ActivationFunctionType
AX = mybir.AxisListType

P = 128
D = 1024
KD = D // P
CTX = 256
SEQ = 256
NT = CTX + SEQ
DEPTH = 2
WF = 512
MB = WF // P
CHUNK = 4
NCH = NT // CHUNK
ST = 64
SG = 16
FF = 2816
FB = FF // P
PARTS = (12, 10)
NE = 8
FE = 3584
FCH = FE // 512
EPS = 1e-6
RING = 3
MRING = 3
SLOT = 4096
NK = CHUNK + 1
TAB = (NK + 1) * 2 * ST
CPW = 4 * CHUNK * P
CKW = CPW + (2 * CHUNK - 1) * P
ADA_TILES = 12 * DEPTH

C_ID, C_ONE, C_TRI, C_BLK, C_IOTA = 0, 128, 256, 384, 512
C_CS, C_CN, C_SN, C_MG, C_MZ, C_SEL = 768, 1024, 1536, 2048, 2050, 2052
C_N = 2054


def constants():
    c = np.zeros((P, C_N), np.float32)
    p = np.arange(P)
    c[:, C_ID:C_ID + P] = np.eye(P)
    c[:, C_ONE:C_ONE + P] = 1.0
    c[:, C_TRI:C_TRI + P] = p[:, None] < p[None, :]
    c[:, C_BLK:C_BLK + P] = (p[:, None] // SG) == (p[None, :] // SG)
    c[:, C_IOTA:C_IOTA + 256] = np.arange(256)
    a = 2 * np.pi * np.outer(p, p) / P
    s = 1.0 / np.sqrt(float(SEQ * P))
    c[:, C_CS:C_CS + P] = np.cos(a) * s
    c[:, C_CS + P:C_CS + 2 * P] = np.sin(a) * s
    t = np.arange(SEQ)
    b = 2 * np.pi * (np.outer(t, t) % SEQ) / SEQ
    c[:, C_CN:C_CN + 512] = np.cos(b).reshape(2, P, SEQ).transpose(1, 0, 2).reshape(P, 512)
    c[:, C_SN:C_SN + 512] = -np.sin(b).reshape(2, P, SEQ).transpose(1, 0, 2).reshape(P, 512)
    for j in range(2):
        c[:, C_MG + j] = (p // SG) % 2 == j
        c[:, C_MZ + j] = p % 2 == j
        c[:, C_SEL + j] = p % 32 == j
    return c


def positions():
    t = np.arange(SEQ)
    q = D // 4
    omega = (1.0 / (np.float32(10000.0) ** (np.arange(q, dtype=np.float32) / np.float32(q)))).astype(np.float32)
    ar = (t // 64).astype(np.float32)[:, None] * omega
    ac = (t % 64).astype(np.float32)[:, None] * omega
    e = np.concatenate([np.sin(ar), np.cos(ar), np.sin(ac), np.cos(ac)], axis=-1).astype(np.float32)
    return np.ascontiguousarray(e.T.reshape(KD, P, SEQ).transpose(1, 0, 2))


def program(nc, a, out, tab, bps, cks):
    top = ExitStack()
    with top:
        def sem(name):
            return top.enter_context(nc.semaphore(name))

        def sb(stack, name, shape, dt=F32):
            return stack.enter_context(nc.sbuf_tensor(name, shape, dt))

        ps = top.enter_context(nc.psum_tensor("ps", [P, 8, 512], F32))

        con = sb(top, "con", [P, C_N])
        hT = sb(top, "hT", [P, KD, NT])
        modv = sb(top, "modv", [P, DEPTH, 48, 2])
        bmod = sb(top, "bmod", [P, DEPTH, 48])
        gains = sb(top, "gains", [P, 5, KD])
        nsc = sb(top, "nsc", [P, 4, KD, 2])
        rms = sb(top, "rms", [P, NT])
        epst = sb(top, "epst", [P, 1])
        L8 = sb(top, "L8", [P, 3, DEPTH * 32])
        wrt = sb(top, "wrt", [P, KD, NE])
        brt = sb(top, "brt", [P, NE])
        dskip = sb(top, "dskip", [P, DEPTH, MB])
        modf = modv[:].rearrange("p l a c -> p (l a) c")
        bmodf = bmod[:].rearrange("p l a -> p (l a)")
        ident = con[:, C_ID:C_ID + P]
        ones = con[:, C_ONE:C_ONE + P]

        inputs_in = sem("inputs_in")
        params_in = sem("params_in")
        landed = [sem(f"landed{i}") for i in range(RING)]
        dve_step = sem("dve_step")
        act_step = sem("act_step")
        silu_c_ready = sem("silu_c_ready")
        tab_ready = sem("tab_ready")
        tab_stored = sem("tab_stored")
        xl_in = [sem(f"xl_in{i}") for i in range(2)]
        bp_free = sem("bp_free")
        cp_free = sem("cp_free")
        kb_free = sem("kb_free")
        mod_bank_zero = sem("mod_bank_zero")
        mod_rows_done = sem("mod_rows_done")
        mod_rows_taken = sem("mod_rows_taken")
        mod_cols_done = sem("mod_cols_done")
        mod_cols_taken = sem("mod_cols_taken")
        bp_made = sem("bp_made")
        bp_masked = sem("bp_masked")
        cp_made = sem("cp_made")
        cp_masked = sem("cp_masked")
        tr_done = sem("tr_done")
        tr_taken = sem("tr_taken")
        taps_done = sem("taps_done")
        kb_made = sem("kb_made")
        l8_done = sem("l8_done")
        l8_masked = sem("l8_masked")
        sq_ready = sem("sq_ready")
        root_ready = sem("root_ready")
        a_block = sem("a_block")
        a_high = sem("a_high")
        w_high = sem("w_high")
        w_low = sem("w_low")
        hid_high = sem("hid_high")
        hid_low = sem("hid_low")
        a_ready = sem("a_ready")
        dense_done = sem("dense_done")
        dense_free = [sem(f"dense_free{i}") for i in range(4)]
        side_done = sem("side_done")
        side_free = [sem(f"side_free{i}") for i in range(4)]
        scan_step = sem("scan_step")
        ys_ready = sem("ys_ready")
        mix_ready = sem("mix_ready")
        out_ready = sem("out_ready")
        out_stored = sem("out_stored")

        dense_order, side_order = [], []
        for l in range(DEPTH):
            dense_order += [("ss", l, 0)]
            dense_order += [("u", l, m) for m in range(4)] + [("f", l, m) for m in range(4)]
            for n in ("ga", "gb", "ya", "glub", "glua", "out"):
                dense_order += [(n, l, m) for m in range(8)]
            dense_order += [("ss", l, 1)]
            if l == 0:
                for part, size in enumerate(PARTS):
                    for m in range(part * PARTS[0], part * PARTS[0] + size):
                        dense_order += [("gate", l, m), ("up", l, m)]
                    dense_order += [("down" + str(part), l, m) for m in range(8)]
            side_order += [("E", l, m, g) for m in range(4) for g in range(4)]
            side_order += [("dft1", l, m, t) for m in range(4) for t in range(2 * l, 4)]
            side_order += [("dft2", l, m, s) for m in range(4) for s in range(l, 2)]
            side_order += [("Y", l, m) for m in range(4)]
        dense_at = {k: i for i, k in enumerate(dense_order)}
        side_at = {k: i for i, k in enumerate(side_order)}

        def place(key):
            if key in dense_at:
                i = dense_at[key]
                return ps[:, i % 4, :], dense_done, dense_free[i % 4], i
            i = side_at[key]
            return ps[:, 4 + i % 4, :], side_done, side_free[i % 4], i

        def bank_for(pe, key):
            bank, _, free, i = place(key)
            if i >= 4:
                pe.wait_ge(free, i // 4)
            return bank

        def arrived(eng, key):
            bank, done, free, i = place(key)
            eng.wait_ge(done, i + 1)
            return bank, free

        def taken(eng, key):
            _, _, free, i = place(key)
            eng.wait_ge(free, i // 4 + 1)

        ffn_tiles = []
        for part, size in enumerate(PARTS):
            first = part * PARTS[0] // 2
            ffn_tiles += [("ffn_gu", 0, n) for n in range(first, first + size // 2)]
            ffn_tiles += [("ffn_down" + str(part), 0, n) for n in range(4)]
        stream = []
        for l in range(DEPTH):
            stream += [("w_in", l, 1), ("w_in", l, 0)]
            stream += [("bp", l, h) for h in range(2)]
            stream += [("w_in", l, n) for n in (2, 3, 4, 5)]
            stream += [("w_four", l, 0)]
            stream += [("ck", l, m) for m in range(4)]
            stream += [("w_glu_b", l, 0), ("w_glu_a", l, 0), ("w_out", l, 0), ("w_out", l, 1)]
            if l == 0:
                stream += ffn_tiles
        ADA = 12 * DEPTH
        stream_at = {k: ADA + i for i, k in enumerate(stream)}

        last_use = {}
        for l in range(DEPTH):
            last_use.update({("w_in", l, 1): ("u", l, 3), ("w_in", l, 0): ("f", l, 3),
                             ("w_in", l, 2): ("ga", l, 3), ("w_in", l, 3): ("ga", l, 7),
                             ("w_in", l, 4): ("gb", l, 3), ("w_in", l, 5): ("gb", l, 7),
                             ("w_four", l, 0): ("ya", l, 7), ("w_glu_b", l, 0): ("glub", l, 7),
                             ("w_glu_a", l, 0): ("glua", l, 7), ("w_out", l, 0): ("out", l, 3),
                             ("w_out", l, 1): ("out", l, 7)})
            last_use.update({("bp", l, h): ("E", l, 2 * h + 1, 3) for h in range(2)})
            last_use.update({("ck", l, m): ("Y", l, m) for m in range(4)})
            for n in range(FB // 2):
                last_use[("ffn_gu", l, n)] = ("up", l, 2 * n + 1)
            for n in range(4):
                for part in range(2):
                    last_use[("ffn_down" + str(part), l, n)] = ("down" + str(part), l, 2 * n + 1)

        moe_order = [("gate", 0), ("up", 0)]
        for c in range(1, FCH):
            moe_order += [("gate", c), ("up", c), ("down", c - 1)]
        moe_order += [("down", FCH - 1)]
        moe_at = {k: i for i, k in enumerate(moe_order)}

        def tile_src(key):
            n, l, i = key
            if n in ("w_in", "w_out"):
                return a[n][l, i]
            if n in ("w_four", "w_glu_a", "w_glu_b"):
                return a[n][l]
            if n[:3] == "ffn":
                return a[n][i]
            if n == "bp":
                return bps[4 * l + 2 * i:4 * l + 2 * i + 2].rearrange("m p c -> p m c")
            return cks[l * 4 + i]

        lows = ExitStack()
        aTl = sb(lows, "aTl", [P, KD, NT], F32R)
        ringl = [sb(lows, f"ringl{i}", [P, SLOT], F32R) for i in range(RING)]
        lows.close()
        early = ExitStack()
        aT = sb(early, "aT", [P, KD, NT])
        ring = [sb(early, f"ring{i}", [P, SLOT]) for i in range(RING)]
        silu_c = sb(early, "silu_c", [P, KD, 2])

        par = ExitStack()
        zt = sb(par, "zt", [P, NK + 1, 2, ST])
        zi = sb(par, "zi", [P, 2, ST])
        ldt = sb(par, "ldt", [P, 1])
        zs = sb(par, "zs", [P, 14, ST])
        zint = sb(par, "zint", [P, ST], I32)
        l8m = sb(par, "l8m", [P, 2, 2, ST])
        XLs = [sb(par, f"XL{i}", [P, 2, NK + 1, 2, ST]) for i in range(2)]
        BCs = [sb(par, f"BC{i}", [P, 2, 2, 2, ST]) for i in range(2)]
        mrow = sb(par, "mrow", [P, 2, 512])
        Bb = sb(par, "Bb", [P, 2, 2, ST])
        t1 = sb(par, "t1", [P, NK, ST])
        t2 = sb(par, "t2", [P, NK, ST])
        t3 = sb(par, "t3", [P, NK, ST])
        t4 = sb(par, "t4", [P, NK, ST])
        BP = sb(par, "BP", [P, 2, 2, CHUNK, ST])
        BPm = sb(par, "BPm", [P, 2, 2, CHUNK, 2, ST])
        CP = sb(par, "CP", [P, 2, 2, NK, ST])
        CPm = sb(par, "CPm", [P, 2, 2, NK, 2, ST])
        CTr = sb(par, "CTr", [P, 2 * 2 * NK + 4, P])
        KB = sb(par, "KB", [P, 2 * CHUNK, P])
        par.close()

        mid = ExitStack()
        ypre = sb(mid, "ypre", [P, 2, NT])
        sg = sb(mid, "sg", [P, 2, NT])
        mix = ExitStack()
        R1 = sb(mix, "R1", [P, 3 * SLOT])
        G = R1[:, 0:SLOT].rearrange("p (k t) -> p k t", k=KD)
        G2 = R1[:, SLOT:2 * SLOT].rearrange("p (k t) -> p k t", k=KD)
        Q = R1[:, 2 * SLOT:3 * SLOT].rearrange("p (a m c) -> p a m c", a=4, m=4)
        ysT = R1[:, 2 * SLOT:2 * SLOT + MB * NT].rearrange("p (m t) -> p m t", m=MB)
        uT = sb(mix, "uT", [P, MB, NT])
        uF = sb(mix, "uF", [P, MB, NT])
        H = sb(mix, "H", [P, NCH + 1, 2, 32])
        sc1 = sb(mix, "sc1", [P, 2, 32])
        sc2 = sb(mix, "sc2", [P, 2, 32])
        mix.close()
        ffn_whole = ExitStack()
        hid = sb(ffn_whole, "hid", [P, max(PARTS), NT])
        ffn_whole.close()
        ffn = ExitStack()
        hidl = sb(ffn, "hidl", [P, max(PARTS), NT], F32R)
        hidh = sb(ffn, "hidh", [P, max(PARTS), NT], F32R)
        FWH = [sb(ffn, f"FWH{i}", [P, SLOT], F32R) for i in range(2)]
        aTh = sb(ffn, "aTh", [P, KD, NT], F32R)
        ffn.close()
        mid.close()
        early.close()

        moe = ExitStack()
        XGh = sb(moe, "XGh", [P, KD, P], F32R)
        XGl = sb(moe, "XGl", [P, KD, P], F32R)
        hTh = sb(moe, "hTh", [P, 2, 4, P], F32R)
        hTl = sb(moe, "hTl", [P, 2, 4, P], F32R)
        mring = [sb(moe, f"mring{i}", [P, SLOT]) for i in range(MRING)]
        WH = [sb(moe, f"WH{i}", [P, SLOT], F32R) for i in range(2)]
        WL = [sb(moe, f"WL{i}", [P, SLOT], F32R) for i in range(2)]
        ftok = sb(moe, "ftok", [P, 2, D])
        lg = sb(moe, "lg", [P, 2, NE])
        mx = sb(moe, "mx", [P, 2, 8])
        mi = sb(moe, "mi", [P, 2, 8], U32)
        mif = sb(moe, "mif", [P, 2, 8])
        wt = sb(moe, "wt", [P, 2, 4])
        oh = sb(moe, "oh", [P, 2, 2, NE])
        sel = sb(moe, "sel", [P, 2, NE])
        comb = sb(moe, "comb", [P, 2, NE + 1])
        rank = sb(moe, "rank", [P, 2, NE + 1])
        cnt = sb(moe, "cnt", [P, 1])
        cnti = sb(moe, "cnti", [P, 1], I32)
        S = sb(moe, "S", [P, 2, P])
        SW = sb(moe, "SW", [P, 2, P])
        SWT = sb(moe, "SWT", [P, 2, SEQ])
        gs = sb(moe, "gs", [P, 2, 512])
        hd = sb(moe, "hd", [P, 2, 512])
        ye = sb(moe, "ye", [P, D])
        fin = ftok[:].rearrange("p a (k t) -> p (a k) t", k=4)
        moe.close()

        mlanded = [sem(f"mlanded{i}") for i in range(MRING)]
        down_done = sem("down_done")
        logits_done = sem("logits_done")
        weights_exp = sem("weights_exp")
        top_ready = sem("top_ready")
        sel_ready = sem("sel_ready")
        rank_done = sem("rank_done")
        rank_ready = sem("rank_ready")
        count_ready = sem("count_ready")
        ftok_done = sem("ftok_done")
        ftok_ready = sem("ftok_ready")
        onehot_ready = sem("onehot_ready")
        scatter_zero = sem("scatter_zero")
        misc_done = sem("misc_done")
        misc_taken = [sem(f"misc_taken{i}") for i in range(2)]
        misc_high = sem("misc_high")
        tile_done = sem("tile_done")
        high_done = sem("high_done")
        low_done = sem("low_done")
        gate_taken = sem("gate_taken")
        hid_ready = sem("hid_ready")
        ye_ready = sem("ye_ready")
        fin_done = sem("fin_done")

        block = top.enter_context(nc.Block())

        misc_order = ([("S", j) for j in range(4)] + [("T", c) for c in range(5)] + [("W", 0), ("T", 5)]
                      + [("G", 0), ("G", 1), ("T", 6)])
        MISC = len(misc_order)
        MISC_PASS = 3 + NE * MISC + 4
        TILES = len(moe_order)
        HALF = SLOT // 2

        def misc_use(pas, e, what):
            if isinstance(e, str) and e == "before":
                k, x = [("G", 0), ("G", 1), ("W", 0)].index(what), 0
            elif isinstance(e, str):
                k, x = 3 + NE * MISC + what[1], 0
            else:
                k, x = 3 + misc_order.index(what), e
            u = pas * MISC_PASS + k
            return u % 2, x * (MISC // 2) + u // 2, x * MISC + u

        @block.sync
        def _(sp):
            sp.dma_start(con[:, :], a["con"]).then_inc(inputs_in, 16)
            for t, n in ((bmod, "bmod"), (gains, "gains"), (dskip, "dskip"), (wrt, "wrt"), (brt, "brt")):
                sp.dma_start(t[:], a[n]).then_inc(inputs_in, 16)
            sp.dma_start(silu_c[:], a["cT"]).then_inc(inputs_in, 16)
            for j in range(RING):
                sp.dma_start(ring[j][:], a["w_mod"][j]).then_inc(landed[j], 16)
            with sp.Fori(1, ADA // RING) as i:
                for j in range(RING):
                    sp.wait_ge(mod_rows_done, i * RING + (j + 1 - RING))
                    sp.dma_start(ring[j][:], a["w_mod"][bass.ds(i * RING + j, 1), :, :]
                                 .rearrange("o p c -> p (o c)")).then_inc(landed[j], 16)
            for key in stream:
                n = stream_at[key]
                if key[0] == "bp" or key[0] == "ck":
                    for s_ in (bp_free,) if key[0] == "bp" else (cp_free, kb_free):
                        sp.wait_ge(s_, 16 * (2 * MB + 1))
                if n - RING < ADA:
                    sp.wait_ge(mod_rows_done, n - RING + 1)
                else:
                    _, done, _, at = place(last_use[stream[n - RING - ADA]])
                    sp.wait_ge(done, at + 1)
                src = tile_src(key)
                dst = ring[n % RING][:, 0:src.shape[-1]]
                if key[0] == "bp":
                    dst = ring[n % RING][:].rearrange("p (m c) -> p m c", m=2)
                sp.dma_start(dst, src).then_inc(landed[n % RING], 16)

            def load(t, e, x):
                kind, c = moe_order[t]
                sp.dma_start(mring[t % MRING][:], a["moe_" + kind][bass.ds(e * FCH + c, 1), :, :]
                             .rearrange("o p c -> p (o c)")).then_inc(mlanded[t % MRING], 16)

            def experts(pas):
                with sp.Fori(0, NE) as e:
                    x = e + NE * pas
                    for t in range(MRING, TILES + MRING):
                        sp.wait_ge(low_done, x * (2 * TILES) + 2 * (t - MRING) + 2)
                        if t < TILES:
                            load(t, e, x)
                        else:
                            load(t - TILES, (e + 1) % NE, x + 1)

            sp.wait_ge(dense_done, dense_at[("out", DEPTH - 1, 7)] + 1)
            for t in range(MRING):
                load(t, 0, 0)
            experts(0)
            sp.wait_ge(mlanded[MRING - 1], 16 * (NE * TILES // MRING + 1))
            sp.wait_ge(count_ready, 1)
            most = sp.value_load(cnti[0:1, 0:1], min_val=0, max_val=SEQ)
            with sp.If(most > P):
                experts(1)
                sp.wait_ge(mlanded[MRING - 1], 16 * (2 * NE * TILES // MRING + 1))
            sp.wait_ge(out_ready, 1)
            sp.dma_start(out, fin).then_inc(out_stored, 16)
            sp.wait_ge(out_stored, 16)

        @block.scalar
        def _(act):
            steps = [0]

            def link(ins):
                steps[0] += 1
                ins.then_inc(act_step, 1)
                act.wait_ge(act_step, steps[0])

            for t, n in ((zi, "lam"), (ldt, "ldt"), (hT, "xT")):
                act.dma_start(t[:], a[n]).then_inc(params_in, 16)
            act.dma_start(aT[:, :, 0:SEQ], a["pos"]).then_inc(params_in, 16)
            act.wait_ge(inputs_in, 7 * 16)
            nc.scalar.activation(silu_c[:], silu_c[:], ACT.Silu).then_inc(silu_c_ready, 1)
            act.wait_ge(tab_ready, 1)
            act.dma_start(tab, zt[:].rearrange("p a b c -> p (a b c)")).then_inc(tab_stored, 16)
            act.wait_ge(tab_stored, 16)
            for s_ in (bp_free, cp_free, kb_free):
                act.sem_inc(s_, 16)

            def load_block(it, h):
                for d in range(2):
                    src = tab[bass.ds(it * 16 + d * 8, 8), :].unsqueeze(1).to_broadcast([8, SG, TAB])
                    act.dma_start(XLs[h][:, d].rearrange("p a b c -> p (a b c)"), src).then_inc(xl_in[h], 16)
                act.dma_start(BCs[h][:].rearrange("p a b c d -> p (a b c d)"),
                              a["bc"][bass.ds(it, 1), :, :].rearrange("o p c -> p (o c)")).then_inc(xl_in[h], 16)

            load_block(0, 0)
            with act.Fori(0, MB) as i:
                for h in range(2):
                    it = i * 2 + h
                    load_block((it + 1) % (2 * MB), 1 - h)
                    for j in range(RING):
                        act.wait_ge(mod_rows_done, it * RING + j + 1)
                        if j >= 2:
                            act.wait_ge(mod_cols_done, it * RING + j - 1)
                        nc.scalar.activation(mrow[:, j % 2, :], ps[:, 6 + j % 2, :], ACT.Copy)\
                            .then_inc(mod_rows_taken, 1)
                    act.wait_ge(bp_made, it + 1)
                    act.wait_ge(bp_free, it * 16 + 16)
                    for b in range(2):
                        nc.scalar.activation(BPm[:].rearrange("p a b k c s -> p (a b k) c s")[:, :, b, :],
                                             BP[:].rearrange("p a b k s -> p (a b k) s"),
                                             ACT.Copy, scale=con[:, C_MG + b:C_MG + b + 1]).then_inc(bp_masked, 1)
                    act.wait_ge(bp_masked, it * 2 + 2)
                    act.dma_start(bps[bass.ds(it, 1), :, :].rearrange("o p c -> p (o c)"),
                                  BPm[:].rearrange("p a b c d e -> p (a b c d e)")).then_inc(bp_free, 16)
                    act.wait_ge(cp_made, it + 1)
                    for b in range(2):
                        nc.scalar.activation(CPm[:].rearrange("p a b k c s -> p (a b k) c s")[:, :, b, :],
                                             CP[:].rearrange("p a b k s -> p (a b k) s"),
                                             ACT.Copy, scale=con[:, C_MG + b:C_MG + b + 1]).then_inc(cp_masked, 1)
                    act.wait_ge(cp_free, it * 16 + 16)
                    for g in range(NK + 1):
                        act.wait_ge(tr_done, it * (NK + 1) + g + 1)
                        nc.scalar.activation(CTr[:, 4 * g:4 * g + 4, :].rearrange("p a c -> p (a c)"),
                                             ps[:, g % 2, :], ACT.Copy).then_inc(tr_taken, 1)
                    act.wait_ge(tr_taken, it * (NK + 1) + (NK + 1))
                    act.dma_start(
                        cks[bass.ds(it, 1), :, 0:CPW].rearrange("o p (a c) -> p (o a) c", a=4),
                        CTr[:, 0:4 * NK, :].rearrange("p (a k) c -> p a (k c)", a=4)[:, :, P:NK * P])\
                        .then_inc(cp_free, 16)
                    act.wait_ge(kb_made, it + 1)
                    act.dma_start(cks[bass.ds(it, 1), :, CPW:CKW].rearrange("o p c -> p (o c)"),
                                  KB[:, 0:2 * CHUNK - 1, :].rearrange("p a c -> p (a c)")).then_inc(kb_free, 16)
            act.wait_ge(xl_in[0], 48 * (MB + 1))
            for s_ in (bp_free, cp_free, kb_free):
                act.wait_ge(s_, 16 * (2 * MB + 1))

            def root(k, l, n):
                bank, free = arrived(act, (k, l, n))
                lo = CTX if (l, n) == (1, 1) else 0
                nc.scalar.activation(rms[:, lo:NT], bank[:, lo:NT], ACT.Sqrt, scale=1.0 / D,
                                     bias=epst[:, 0:1]).then_inc(free, 1)

            def evac(key, dst, func=ACT.Copy, cols=NT):
                bank, free = arrived(act, key)
                nc.scalar.activation(dst, bank[:, 0:cols], func).then_inc(free, 1)

            def weights_high(i):
                if i >= len(ffn_tiles):
                    return
                if i >= 2:
                    _, done, _, at = place(last_use[ffn_tiles[i - 2]])
                    act.wait_ge(done, at + 1)
                n_ = stream_at[ffn_tiles[i]]
                act.wait_ge(landed[n_ % RING], 16 * (n_ // RING + 1))
                w_ = tile_src(ffn_tiles[i]).shape[-1]
                nc.scalar.activation(FWH[i % 2][:, 0:w_], ring[n_ % RING][:, 0:w_], ACT.Copy).then_inc(w_high, 1)

            def hidden_high(m, m0):
                taken(act, ("up", 0, m))
                nc.scalar.activation(hidh[:, m - m0, :], hid[:, m - m0, :], ACT.Copy).then_inc(hid_high, 1)

            def shift(l, n_):
                lo = CTX if (l, n_) == (1, 1) else 0
                split = (l, n_) == (0, 1)
                for kk in range(KD):
                    act.wait_ge(a_block, KD * (2 * l + n_) + kk + 1)
                    for s_ in range(lo // CTX, 2):
                        v = slice(256 * s_, 256 * s_ + 256)
                        last = nc.scalar.activation((aTh if split else aT)[:, kk, v], aT[:, kk, v], ACT.Identity,
                                                    bias=modv[:, l, 24 * n_ + kk, s_:s_ + 1])
                    last.then_inc(a_high if split else a_ready, 1)

            for l in range(DEPTH):
                t0 = CTX * l
                n = NT - t0
                root("ss", l, 0)
                shift(l, 0)
                for m in range(4):
                    evac(("u", l, m), uT[:, m, :])
                for m in range(4):
                    evac(("f", l, m), uF[:, m, t0:NT], cols=n)
                for m in range(4):
                    for t in range(2 * l, 4):
                        evac(("dft1", l, m, t), Q[:, t, m, :], cols=2 * P)
                for m in range(4):
                    for s in range(l, 2):
                        evac(("dft2", l, m, s), uF[:, m, s * 256:s * 256 + 256], cols=256)
                for m in range(8):
                    evac(("ga", l, m), G[:, m, t0:NT], ACT.Sigmoid, n)
                for m in range(8):
                    evac(("gb", l, m), G2[:, m, t0:NT], ACT.Sigmoid, n)
                for m in range(4):
                    act.wait_ge(side_free[side_at[("Y", l, m)] % 4], side_at[("Y", l, m)] // 4 + 1)
                    nc.scalar.activation(ysT[:, m, t0:NT], ypre[:, m % 2, t0:NT],
                                         ACT.Gelu_apprx_tanh).then_inc(ys_ready, 1)
                for m in range(8):
                    evac(("glub", l, m), aT[:, m, t0:NT], ACT.Sigmoid, n)
                if l == 0:
                    weights_high(0)
                    weights_high(1)
                root("ss", l, 1)
                shift(l, 1)
                if l == 0:
                    ahead = 2
                    for part, size in enumerate(PARTS):
                        m0 = part * PARTS[0]
                        for m in range(m0, m0 + size):
                            if m - m0 >= 2:
                                taken(act, ("up", l, m - 2))
                            evac(("gate", l, m), sg[:, m % 2, :], ACT.Silu)
                            if m > m0:
                                hidden_high(m - 1, m0)
                            if m % 2:
                                if m == m0 + size - 1:
                                    hidden_high(m, m0)
                                weights_high(ahead)
                                ahead += 1
                        for t in range(4):
                            weights_high(ahead)
                            ahead += 1

            act.sem_inc(ye_ready, 2)
            act.wait_ge(top_ready, 1)
            nc.scalar.activation(wt[:, :, 1:2], wt[:, :, 0:1], ACT.Exp).then_inc(weights_exp, 1)
            for g in range(4):
                act.wait_ge(ftok_done, g + 1)
                nc.scalar.activation(ftok[:, g // 2, (g % 2) * 512:(g % 2) * 512 + 512], ps[:, g, :],
                                     ACT.Copy).then_inc(ftok_ready, 1)

            def split(t, buf, x):
                if t >= TILES:
                    t, x = t - TILES, x + 1
                act.wait_ge(mlanded[t % MRING], x * (16 * TILES // MRING) + 16 * (t // MRING + 1))
                for h in range(2):
                    o = slice(HALF * h, HALF * h + HALF)
                    nc.scalar.activation(WH[buf][:, o], mring[t % MRING][:, o], ACT.Copy).then_inc(high_done, 1)

            def take_high(pas, e, what, dst):
                b, _, u = misc_use(pas, e, what)
                act.wait_ge(misc_done, u + 1)
                nc.scalar.activation(dst, ps[:, 6 + b, :], ACT.Copy).then_inc(misc_high, 1)

            def take_weights(pas, e, par):
                b, _, u = misc_use(pas, e, ("W", 0))
                act.wait_ge(misc_done, u + 1)
                nc.scalar.activation(SWT[:, par, :], ps[:, 6 + b, 0:SEQ], ACT.Copy).then_inc(misc_taken[b], 1)

            def xg_high(g):
                return XGh[:, 4 * g:4 * g + 4, :].rearrange("p a c -> p (a c)")

            def experts(pas):
                for g in range(2):
                    take_high(pas, "before", ("G", g), xg_high(g))
                take_weights(pas, "before", 0)
                if pas == 0:
                    split(0, 0, 0)
                    split(1, 1, 0)
                with act.Fori(0, NE // 2) as i:
                    for par in range(2):
                        e = i * 2 + par
                        x = e + NE * pas
                        for t, (kind, c) in enumerate(moe_order):
                            act.wait_ge(tile_done, x * TILES + t + 1)
                            if kind == "gate":
                                if c >= 2:
                                    act.wait_ge(hid_ready, x * FCH + c - 1)
                                nc.scalar.activation(gs[:, c % 2, :], ps[:, 2 * (c % 2), :], ACT.Silu)\
                                    .then_inc(gate_taken, 1)
                                if c >= 1:
                                    take_high(pas, e, ("T", c - 1), hTh[:, (c - 1) % 2].rearrange("p a c -> p (a c)"))
                            if (kind, c) == ("up", 5):
                                take_weights(pas, e, 1 - par)
                            if (kind, c) == ("up", 6):
                                for g in range(2):
                                    take_high(pas, e, ("G", g), xg_high(g))
                                take_high(pas, e, ("T", 6), hTh[:, 0].rearrange("p a c -> p (a c)"))
                            if (kind, c) == ("down", 6):
                                for h in range(2):
                                    nc.scalar.activation(ye[:, 512 * h:512 * h + 512], ps[:, 4 + h, :],
                                                         ACT.Copy).then_inc(ye_ready, 1)
                            split(t + 2, (par + t) % 2, x)
            experts(0)
            act.wait_ge(count_ready, 1)
            most = act.value_load(cnti[0:1, 0:1], min_val=0, max_val=SEQ)
            with act.If(most > P):
                experts(1)
            act.wait_ge(fin_done, 1)
            nc.scalar.activation(rms[:, 0:SEQ], ps[:, 0, 0:SEQ], ACT.Sqrt, scale=1.0 / D,
                                 bias=epst[:, 0:1]).then_inc(root_ready, 1)

        @block.vector
        def _(dve):
            V = nc.vector
            steps = [0]

            def link(ins):
                steps[0] += 1
                ins.then_inc(dve_step, 1)
                dve.wait_ge(dve_step, steps[0])

            link(V.memset(epst[:], EPS))
            dve.wait_ge(params_in, 4 * 16)
            link(V.tensor_tensor(hT[:, :, CTX:NT], hT[:, :, CTX:NT], aT[:, :, 0:SEQ], ALU.add))

            z = [zs[:, k, :] for k in range(14)]
            BIG = 12582912.0

            def exp_to(dst, x, n, r, w, ti, cols):
                c = slice(0, cols)
                link(V.tensor_scalar(n[:, c], x, -87.0, 88.0, ALU.max, ALU.min))
                link(V.tensor_copy(w[:, c], n[:, c]))
                link(V.tensor_scalar(n[:, c], n[:, c], 1.4426950408889634, BIG, ALU.mult, ALU.add))
                link(V.tensor_scalar(n[:, c], n[:, c], BIG, None, ALU.subtract))
                link(V.scalar_tensor_tensor(w[:, c], n[:, c], -0.693359375, w[:, c], ALU.mult, ALU.add))
                link(V.scalar_tensor_tensor(r[:, c], n[:, c], 2.12194440e-4, w[:, c], ALU.mult, ALU.add))
                link(V.tensor_scalar(n[:, c], n[:, c], 127.0, 8388608.0, ALU.add, ALU.mult))
                link(V.tensor_copy(ti[:, c], n[:, c]))
                link(V.tensor_scalar(w[:, c], r[:, c], 1.0 / 5040, None, ALU.mult))
                for k in (720, 120, 24, 6, 2, 1):
                    link(V.scalar_tensor_tensor(w[:, c], w[:, c], 1.0 / k, r[:, c], ALU.add, ALU.mult))
                link(V.tensor_scalar(w[:, c], w[:, c], 1.0, None, ALU.add))
                link(V.tensor_tensor(w[:, c], w[:, c], ti[:, c].bitcast(F32), ALU.mult))
                link(V.tensor_scalar(n[:, c], x, -87.0, None, ALU.is_ge))
                link(V.tensor_tensor(dst, w[:, c], n[:, c], ALU.mult))

            are, aim = zi[:, 0, :], zi[:, 1, :]
            exp_to(z[0][:, 0:1], ldt[:, 0:1], z[1], z[2], z[3], zint, 1)
            dt = z[0][:, 0:1]
            link(V.tensor_scalar(z[4], are, dt, None, ALU.mult))
            link(V.tensor_scalar(z[5], aim, dt, None, ALU.mult))
            exp_to(z[6], z[4], z[1], z[2], z[3], zint, ST)
            n, r, r2, s, c, qa, qb, w = z[1], z[2], z[3], z[7], z[8], z[9], z[10], z[11]
            link(V.tensor_scalar(n, z[5], 0.6366197723675814, BIG, ALU.mult, ALU.add))
            link(V.tensor_scalar(n, n, BIG, None, ALU.subtract))
            link(V.scalar_tensor_tensor(r, n, -1.5703125, z[5], ALU.mult, ALU.add))
            link(V.scalar_tensor_tensor(r, n, -4.837512969970703125e-4, r, ALU.mult, ALU.add))
            link(V.scalar_tensor_tensor(r, n, -7.54978995489188216e-8, r, ALU.mult, ALU.add))
            link(V.tensor_tensor(r2, r, r, ALU.mult))
            link(V.tensor_scalar(s, r2, 1.0 / 362880, None, ALU.mult))
            for k in (-1.0 / 5040, 1.0 / 120, -1.0 / 6):
                link(V.scalar_tensor_tensor(s, s, k, r2, ALU.add, ALU.mult))
            link(V.scalar_tensor_tensor(s, s, 1.0, r, ALU.add, ALU.mult))
            link(V.tensor_scalar(c, r2, -1.0 / 3628800, None, ALU.mult))
            for k in (1.0 / 40320, -1.0 / 720, 1.0 / 24, -0.5):
                link(V.scalar_tensor_tensor(c, c, k, r2, ALU.add, ALU.mult))
            link(V.tensor_scalar(c, c, 1.0, None, ALU.add))
            link(V.tensor_scalar(w, n, 0.25, BIG, ALU.mult, ALU.add))
            link(V.tensor_scalar(w, w, BIG, None, ALU.subtract))
            link(V.scalar_tensor_tensor(n, w, -4.0, n, ALU.mult, ALU.add))
            link(V.tensor_tensor(w, n, n, ALU.mult))
            link(V.tensor_scalar(qb, w, 4.0, None, ALU.is_equal))
            link(V.tensor_scalar(qa, n, 0.0, None, ALU.is_equal))
            link(V.tensor_tensor(qa, qa, qb, ALU.subtract))
            link(V.tensor_scalar(qb, n, 1.0, None, ALU.is_equal))
            link(V.tensor_scalar(w, n, -1.0, None, ALU.is_equal))
            link(V.tensor_tensor(qb, qb, w, ALU.subtract))
            er = z[6]
            lr, li = zt[:, 1, 0, :], zt[:, 1, 1, :]
            link(V.tensor_tensor(w, qa, c, ALU.mult))
            link(V.tensor_tensor(z[12], qb, s, ALU.mult))
            link(V.tensor_tensor(w, w, z[12], ALU.subtract))
            link(V.tensor_tensor(lr, w, er, ALU.mult))
            link(V.tensor_tensor(w, qa, s, ALU.mult))
            link(V.tensor_tensor(z[12], qb, c, ALU.mult))
            link(V.tensor_tensor(w, w, z[12], ALU.add))
            link(V.tensor_tensor(li, w, er, ALU.mult))
            link(V.memset(zt[:, 0, 0, :], 1.0))
            link(V.memset(zt[:, 0, 1, :], 0.0))

            def power(k0, k1, by):
                cnt_ = k1 - k0 + 1
                A_r, A_i = zt[:, k0:k1 + 1, 0, :], zt[:, k0:k1 + 1, 1, :]
                b_r = zt[:, by:by + 1, 0, :].to_broadcast([P, cnt_, ST])
                b_i = zt[:, by:by + 1, 1, :].to_broadcast([P, cnt_, ST])
                x1, x2, x3, x4 = (t[:, 0:cnt_, :] for t in (t1, t2, t3, t4))
                V.tensor_tensor(x1, A_r, b_r, ALU.mult)
                V.tensor_tensor(x2, A_i, b_i, ALU.mult)
                V.tensor_tensor(x3, A_r, b_i, ALU.mult)
                link(V.tensor_tensor(x4, A_i, b_r, ALU.mult))
                V.tensor_tensor(zt[:, k0 + by:k1 + by + 1, 0, :], x1, x2, ALU.subtract)
                link(V.tensor_tensor(zt[:, k0 + by:k1 + by + 1, 1, :], x3, x4, ALU.add))
            power(1, 1, 1)
            power(1, 2, 2)
            l1, d1, d2 = z[12], z[1], z[2]
            link(V.tensor_scalar(l1, lr, 1.0, None, ALU.subtract))
            link(V.tensor_tensor(d1, are, are, ALU.mult))
            link(V.tensor_tensor(d2, aim, aim, ALU.mult))
            link(V.tensor_tensor(d1, d1, d2, ALU.add))
            link(V.reciprocal(d1, d1))
            link(V.tensor_tensor(z[3], l1, are, ALU.mult))
            link(V.tensor_tensor(z[7], li, aim, ALU.mult))
            link(V.tensor_tensor(z[3], z[3], z[7], ALU.add))
            link(V.tensor_tensor(zt[:, NK, 0, :], z[3], d1, ALU.mult))
            link(V.tensor_tensor(z[3], li, are, ALU.mult))
            link(V.tensor_tensor(z[7], l1, aim, ALU.mult))
            link(V.tensor_tensor(z[3], z[3], z[7], ALU.subtract))
            V.tensor_tensor(zt[:, NK, 1, :], z[3], d1, ALU.mult).then_inc(tab_ready, 1)
            dve.wait_ge(inputs_in, 7 * 16)
            for b in range(2):
                last = V.tensor_scalar(l8m[:, :, b, :], zt[:, CHUNK, :, :], con[:, C_MZ + b:C_MZ + b + 1],
                                       None, ALU.mult)
            last.then_inc(l8_masked, 1)
            dve.wait_ge(l8_done, 1)
            for k in range(2):
                link(V.tensor_copy(t1[:, 0:2, :].rearrange("p a c -> p (a c)"), ps[:, k, 0:P]))
                v = t1[:, 0:2, :].rearrange("p a (c b) -> p (a c) b", b=2)
                link(V.tensor_tensor(L8[:, k, :], v[:, :, 0], v[:, :, 1], ALU.add))
            link(V.tensor_scalar(L8[:, 2, :], L8[:, 1, :], -1.0, None, ALU.mult))

            for b in range(2):
                last = V.memset(ps[:, 6 + b, :], 0.0)
            last.then_inc(mod_bank_zero, 1)

            base = steps[0]
            PER = 11
            with dve.Fori(0, MB) as i2:
              for h in range(2):
                i = i2 * 2 + h
                XL, BC = XLs[h], BCs[h]
                k = 0

                def step(ins):
                    nonlocal k
                    k += 1
                    ins.then_inc(dve_step, 1)
                    dve.wait_ge(dve_step, base + i * PER + k)

                def two(o1, o2, ar, ai, br, bi, x, neg=False):
                    V.tensor_tensor(x[0], ar, br, ALU.mult)
                    V.tensor_tensor(x[1], ai, bi, ALU.mult)
                    V.tensor_tensor(x[2], ar, bi, ALU.mult)
                    step(V.tensor_tensor(x[3], ai, br, ALU.mult))
                    V.tensor_tensor(o1, x[0], x[1], ALU.subtract)
                    return V.tensor_tensor(o2, x[2], x[3], ALU.add)

                dve.wait_ge(xl_in[h], i2 * 48 + 48)
                wr, wi = XL[:, :, NK, 0, :], XL[:, :, NK, 1, :]
                x = [t[:, 0:2, :] for t in (t1, t2, t3, t4)]
                step(two(Bb[:, :, 0, :], Bb[:, :, 1, :], wr, wi, BC[:, 0, :, 0, :], BC[:, 0, :, 1, :], x))
                for d in range(2):
                    br = Bb[:, d, 0:1, :].to_broadcast([P, CHUNK, ST])
                    bi = Bb[:, d, 1:2, :].to_broadcast([P, CHUNK, ST])
                    x = [t[:, 0:CHUNK, :] for t in (t1, t2, t3, t4)]
                    ins = two(BP[:, d, 0], BP[:, d, 1], XL[:, d, 0:CHUNK, 0, :], XL[:, d, 0:CHUNK, 1, :], br, bi, x)
                    if d == 0:
                        step(ins)
                ins.then_inc(bp_made, 1)
                dve.wait_ge(bp_made, i + 1)
                for d in range(2):
                    cr = BC[:, 1, d, 0:1, :].to_broadcast([P, NK, ST])
                    ci = BC[:, 1, d, 1:2, :].to_broadcast([P, NK, ST])
                    x = [t[:] for t in (t1, t2, t3, t4)]
                    step(two(CP[:, d, 0], CP[:, d, 1], XL[:, d, 0:NK, 0, :], XL[:, d, 0:NK, 1, :], cr, ci, x))
                V.tensor_scalar(CP[:, :, 1].rearrange("p a k s -> p a (k s)"),
                                CP[:, :, 1].rearrange("p a k s -> p a (k s)"), -1.0, None,
                                ALU.mult).then_inc(cp_made, 1)
                dve.wait_ge(kb_free, i * 16 + 16)
                dve.wait_ge(taps_done, i + 1)
                blk = con[:, C_BLK:C_BLK + P].unsqueeze(1).to_broadcast([P, CHUNK, P])
                for d in range(2):
                    ins = V.tensor_tensor(KB[:, CHUNK * d:CHUNK * d + CHUNK, :],
                                          ps[:, 2 + d, :].rearrange("p (k c) -> p k c", k=CHUNK), blk, ALU.mult)
                step(ins)
                step(V.tensor_tensor(KB[:, 0, :], KB[:, 0, :], KB[:, CHUNK, :], ALU.add))
                V.tensor_copy(KB[:, CHUNK, :], KB[:, 2 * CHUNK - 1, :]).then_inc(kb_made, 1)
                for j in range(RING):
                    n = i * RING + j
                    dve.wait_ge(mod_cols_done, n + 1)
                    V.tensor_tensor(modf[:, bass.ds(n * 4, 4), :],
                                    ps[:, 4, 8 * j:8 * j + 8].rearrange("p (a c) -> p a c", c=2),
                                    bmodf[:, bass.ds(n * 4, 4)].unsqueeze(2).to_broadcast([P, 4, 2]),
                                    ALU.add).then_inc(mod_cols_taken, 1)
                assert k == PER, k
            steps[0] = base + PER * 2 * MB

            dve.wait_ge(xl_in[0], 48 * (MB + 1))
            for s_ in (bp_free, cp_free, kb_free):
                dve.wait_ge(s_, 16 * (2 * MB + 1))
            dve.wait_ge(mod_cols_taken, ADA)
            for l in range(DEPTH):
                for n_, o in ((0, 8), (1, 32)):
                    link(V.tensor_scalar(nsc[:, 2 * l + n_], modv[:, l, o:o + 8, :], 1.0, None, ALU.add))
                    link(V.tensor_tensor(nsc[:, 2 * l + n_], nsc[:, 2 * l + n_],
                                         gains[:, 2 * l + n_, :].unsqueeze(2).to_broadcast([P, KD, 2]), ALU.mult))

            def square(m, lo):
                V.tensor_tensor(aT[:, m, lo:NT], hT[:, m, lo:NT], hT[:, m, lo:NT], ALU.mult).then_inc(sq_ready, 1)

            def norm(l, n_):
                lo = CTX if (l, n_) == (1, 1) else 0
                taken(dve, ("ss", l, n_))
                link(V.reciprocal(rms[:, lo:NT], rms[:, lo:NT]))
                for kk in range(KD):
                    for s_ in range(lo // CTX, 2):
                        v = slice(256 * s_, 256 * s_ + 256)
                        last = V.scalar_tensor_tensor(aT[:, kk, v], hT[:, kk, v], nsc[:, 2 * l + n_, kk, s_:s_ + 1],
                                                      rms[:, v], ALU.mult, ALU.mult)
                    last.then_inc(a_block, 1)
                if (l, n_) == (0, 1):
                    for kk in range(KD):
                        dve.wait_ge(a_high, kk + 1)
                        for s_ in range(2):
                            v = slice(256 * s_, 256 * s_ + 256)
                            last = V.scalar_tensor_tensor(aTl[:, kk, v], aT[:, kk, v], modv[:, 0, 24 + kk, s_:s_ + 1],
                                                          aTh[:, kk, v].bitcast(F32), ALU.add, ALU.subtract)
                        last.then_inc(a_ready, 1)

            def weights_low(i):
                if i < len(ffn_tiles):
                    s_, w_ = stream_at[ffn_tiles[i]] % RING, tile_src(ffn_tiles[i]).shape[-1]
                    dve.wait_ge(w_high, i + 1)
                    V.tensor_tensor(ringl[s_][:, 0:w_], ring[s_][:, 0:w_], FWH[i % 2][:, 0:w_].bitcast(F32),
                                    ALU.subtract).then_inc(w_low, 1)

            def hidden_low(m, m0):
                dve.wait_ge(hid_high, m + 1)
                V.tensor_tensor(hidl[:, m - m0, :], hid[:, m - m0, :],
                                hidh[:, m - m0, :].bitcast(F32), ALU.subtract).then_inc(hid_low, 1)

            def residual(key, l, m, gate, lo, squares=True):
                bank, free = arrived(dve, key)
                for s_ in range(lo // CTX, 2):
                    v = hT[:, m, 256 * s_:256 * s_ + 256]
                    last = V.scalar_tensor_tensor(v, bank[:, 256 * s_ - lo:256 * s_ - lo + 256],
                                                  modv[:, l, gate + m, s_:s_ + 1], v, ALU.mult, ALU.add)
                last.then_inc(free, 1)
                if squares:
                    taken(dve, key)
                    square(m, lo)

            scans = [0]
            for l in range(DEPTH):
                t0 = CTX * l
                n_ = NT - t0
                if l == 0:
                    for m in range(KD):
                        square(m, 0)
                norm(l, 0)
                link(V.memset(H[:, 0], 0.0))
                for m in range(4):
                    for g in range(4):
                        bank, free = arrived(dve, ("E", l, m, g))
                        ev = bank[:, 0:4 * NCH].rearrange("p (d r c) -> p d c r", d=2, r=2)
                        col = m * 8 + g
                        V.tensor_copy(H[:, 1:NCH + 1, :, col], ev[:, 0])
                        V.tensor_copy(H[:, 1:NCH + 1, :, col + 4].rearrange("p (s c) r -> p s c r", s=2),
                                      ev[:, 1].rearrange("p (s c) r -> p s c r", s=2)[:, :, ::-1, :]).then_inc(free, 1)
                taken(dve, ("E", l, 3, 3))
                l8r = L8[:, 0:1, 32 * l:32 * l + 32].to_broadcast([P, 2, 32])
                l8x = L8[:, 1:3, 32 * l:32 * l + 32]
                UN = 8
                sb0 = scans[0]
                with dve.Fori(0, NCH // UN) as i:
                    for u in range(UN):
                        now = H[:, bass.ds(i * UN + u, 1), :, :].rearrange("p o r c -> p (o r) c")
                        nxt = H[:, bass.ds(i * UN + (u + 1), 1), :, :].rearrange("p o r c -> p (o r) c")
                        if u:
                            dve.wait_ge(scan_step, sb0 + i * (4 * UN) + 4 * u)
                        V.tensor_tensor(sc1[:], now, l8r, ALU.mult).then_inc(scan_step, 1)
                        V.tensor_tensor(sc2[:, ::-1, :], now, l8x, ALU.mult).then_inc(scan_step, 1)
                        dve.wait_ge(scan_step, sb0 + i * (4 * UN) + 4 * u + 1)
                        V.tensor_tensor(sc1[:], sc1[:], nxt, ALU.add).then_inc(scan_step, 1)
                        dve.wait_ge(scan_step, sb0 + i * (4 * UN) + 4 * u + 3)
                        V.tensor_tensor(nxt, sc1[:], sc2[:], ALU.add).then_inc(scan_step, 1)
                    dve.wait_ge(scan_step, sb0 + i * (4 * UN) + 4 * UN)
                scans[0] = sb0 + 4 * NCH
                for m in range(8):
                    taken(dve, ("ga", l, m))
                    bank, free = arrived(dve, ("ya", l, m))
                    V.tensor_tensor(G[:, m, t0:NT], G[:, m, t0:NT], bank[:, 0:n_], ALU.mult).then_inc(free, 1)
                for m in range(4):
                    if m >= 2:
                        dve.wait_ge(ys_ready, 4 * l + m - 1)
                    bank, free = arrived(dve, ("Y", l, m))
                    V.scalar_tensor_tensor(ypre[:, m % 2, t0:NT], uT[:, m, t0:NT], dskip[:, l, m:m + 1],
                                           bank[:, 0:n_], ALU.mult, ALU.add).then_inc(free, 1)
                for m in range(8):
                    taken(dve, ("glub", l, m))
                    taken(dve, ("gb", l, m))
                    bank, free = arrived(dve, ("glua", l, m))
                    V.tensor_tensor(aT[:, m, t0:NT], aT[:, m, t0:NT], bank[:, 0:n_], ALU.mult).then_inc(free, 1)
                    taken(dve, ("glua", l, m))
                    link(V.tensor_tensor(G2[:, m, t0:NT], G2[:, m, t0:NT], aT[:, m, t0:NT], ALU.mult))
                    V.tensor_tensor(G[:, m, t0:NT], G[:, m, t0:NT], G2[:, m, t0:NT], ALU.add).then_inc(mix_ready, 1)
                for m in range(8):
                    residual(("out", l, m), l, m, 16, t0)
                    if l == 0 and m in (3, 6):
                        weights_low(m // 5)
                norm(l, 1)
                if l == 0:
                    ahead = 2
                    for part, size in enumerate(PARTS):
                        m0 = part * PARTS[0]
                        for m in range(m0, m0 + size):
                            taken(dve, ("gate", l, m))
                            bank, free = arrived(dve, ("up", l, m))
                            V.tensor_tensor(hid[:, m - m0, :], sg[:, m % 2, :], bank[:, 0:NT], ALU.mult).then_inc(free, 1)
                            if m > m0:
                                hidden_low(m - 1, m0)
                            if m % 2:
                                if m == m0 + size - 1:
                                    hidden_low(m, m0)
                                weights_low(ahead)
                                ahead += 1
                        for m in range(8):
                            residual(("down" + str(part), l, m), l, m, 40, 0, part == 1)
                            if m % 2:
                                weights_low(ahead)
                                ahead += 1
                    taken(dve, ("down1", l, 7))

            dve.wait_ge(logits_done, 1)
            link(V.tensor_tensor(lg[:], ps[:, 7, 0:16].rearrange("p (a e) -> p a e", a=2),
                                 brt[:].unsqueeze(1).to_broadcast([P, 2, NE]), ALU.add))
            for t in range(2):
                link(V.max(mx[:, t, :], lg[:, t, :]))
                link(V.max_index(mi[:, t, :], mx[:, t, :], lg[:, t, :]))
            link(V.tensor_copy(mif[:], mi[:]))
            V.tensor_tensor(wt[:, :, 0:1], mx[:, :, 1:2], mx[:, :, 0:1], ALU.subtract).then_inc(top_ready, 1)
            iota = con[:, C_IOTA:C_IOTA + 256]
            for t in range(2):
                for j in range(2):
                    link(V.tensor_scalar(oh[:, t, j, :], iota[:, 0:NE], mif[:, t, j:j + 1], None, ALU.is_equal))
            V.tensor_tensor(sel[:], oh[:, :, 0, :], oh[:, :, 1, :], ALU.add).then_inc(sel_ready, 1)
            dve.wait_ge(weights_exp, 1)
            link(V.tensor_scalar(wt[:, :, 2:3], wt[:, :, 1:2], 1.0, None, ALU.add))
            link(V.reciprocal(wt[:, :, 2:3], wt[:, :, 2:3]))
            link(V.tensor_tensor(wt[:, :, 3:4], wt[:, :, 1:2], wt[:, :, 2:3], ALU.mult))
            for t in range(2):
                link(V.tensor_scalar(comb[:, t, 0:NE], oh[:, t, 0, :], wt[:, t, 2:3], None, ALU.mult))
                link(V.scalar_tensor_tensor(comb[:, t, 0:NE], oh[:, t, 1, :], wt[:, t, 3:4], comb[:, t, 0:NE],
                                            ALU.mult, ALU.add))
            dve.wait_ge(rank_done, 1)
            link(V.memset(rank[:], 4096.0))
            link(V.memset(comb[:, :, NE:NE + 1], 0.0))
            link(V.tensor_scalar(rank[:, :, 0:NE], sel[:], -4096.0, 4096.0, ALU.mult, ALU.add))
            link(V.tensor_tensor(rank[:, :, 0:NE], rank[:, :, 0:NE], ps[:, 7, 16:32].rearrange("p (a e) -> p a e", a=2), ALU.add))
            link(V.reduce_max(cnt[:], ps[:, 7, 32:40], AX.X))
            V.tensor_copy(cnti[:], cnt[:]).then_inc(count_ready, 1)

            def onehot(pas, e):
                slots = iota[:, P * pas:P * pas + P]
                for t in range(2):
                    V.tensor_scalar(S[:, t, :], slots, rank[:, t, bass.ds(e, 1)], None, ALU.is_equal)
                    last = V.tensor_scalar(SW[:, t, :], slots, rank[:, t, bass.ds(e, 1)],
                                           comb[:, t, bass.ds(e, 1)], ALU.is_equal, ALU.mult)
                last.then_inc(onehot_ready, 1)

            def split(t, buf, x):
                if t >= TILES:
                    t, x = t - TILES, x + 1
                for h in range(2):
                    o = slice(HALF * h, HALF * h + HALF)
                    dve.wait_ge(high_done, x * (2 * TILES) + 2 * t + h + 1)
                    V.tensor_tensor(WL[buf][:, o], mring[t % MRING][:, o], WH[buf][:, o].bitcast(F32),
                                    ALU.subtract).then_inc(low_done, 1)

            def take_low(pas, e, what, x, high, low):
                b, _, u = misc_use(pas, e, what)
                n = (2 + NE * len(highs)) * pas
                n = n + what[1] + 1 if isinstance(e, str) else e * len(highs) + (n + 3 + highs.index(what))
                dve.wait_ge(misc_high, n)
                V.tensor_tensor(low, ps[:, 6 + b, :], high.bitcast(F32), ALU.subtract).then_inc(misc_taken[b], 1)

            highs = [m_ for m_ in misc_order if m_[0] in "TG"]

            def scatter(pas, e, j):
                b, _, u = misc_use(pas, e, ("S", j))
                dve.wait_ge(misc_done, u + 1)
                for i_ in range(2):
                    v = hT[:, 2 * j + i_, CTX:NT]
                    last = V.scalar_tensor_tensor(v, ps[:, 6 + b, 256 * i_:256 * i_ + 256],
                                                  modv[:, 1, 40 + 2 * j + i_, 1:2], v, ALU.mult, ALU.add)
                last.then_inc(misc_taken[b], 1)

            def xg(t_, g):
                return t_[:, 4 * g:4 * g + 4, :].rearrange("p a c -> p (a c)")

            def ht(t_, c):
                return t_[:, c % 2].rearrange("p a c -> p (a c)")

            def experts(pas):
                V.memset(ye[:], 0.0)
                V.memset(SWT[:, 1, :], 0.0).then_inc(scatter_zero, 1)
                onehot(pas, 0)
                for g in range(2):
                    take_low(pas, "before", ("G", g), None, xg(XGh, g), xg(XGl, g))
                if pas == 0:
                    split(0, 0, 0)
                    split(1, 1, 0)
                with dve.Fori(0, NE // 2) as i:
                    for par in range(2):
                        e = i * 2 + par
                        x = e + NE * pas
                        for t, (kind, c) in enumerate(moe_order):
                            if kind == "gate" and c >= 1:
                                take_low(pas, e, ("T", c - 1), x, ht(hTh, c - 1), ht(hTl, c - 1))
                            if (kind, c) == ("gate", 0):
                                for j in range(2):
                                    scatter(pas, e, j)
                            if kind == "up":
                                dve.wait_ge(gate_taken, x * FCH + c + 1)
                                dve.wait_ge(tile_done, x * TILES + t + 1)
                                if c >= 2:
                                    dve.wait_ge(misc_done, misc_use(pas, e, ("T", c - 2))[2] + 1)
                                V.tensor_tensor(hd[:, c % 2, :], gs[:, c % 2, :], ps[:, 2 * (c % 2) + 1, :],
                                                ALU.mult).then_inc(hid_ready, 1)
                            if (kind, c) == ("up", 0):
                                for j in range(2, 4):
                                    scatter(pas, e, j)
                            if (kind, c) == ("up", 1):
                                onehot(pas, e + 1)
                            if (kind, c) == ("up", 6):
                                for g in range(2):
                                    take_low(pas, e, ("G", g), x, xg(XGh, g), xg(XGl, g))
                                take_low(pas, e, ("T", 6), x, ht(hTh, 6), ht(hTl, 6))
                            split(t + 2, (par + t) % 2, x)
                for j in range(4):
                    scatter(pas, "after", j)
                b, n, _ = misc_use(pas, "after", ("S", 3))
                dve.wait_ge(misc_taken[b], n + 1)
            experts(0)
            most = dve.value_load(cnti[0:1, 0:1], min_val=0, max_val=SEQ)
            with dve.If(most > P):
                experts(1)
            V.tensor_tensor(fin, hT[:, :, CTX:NT], hT[:, :, CTX:NT], ALU.mult).then_inc(sq_ready, 1)
            dve.wait_ge(root_ready, 1)
            link(V.reciprocal(rms[:, 0:SEQ], rms[:, 0:SEQ]))
            link(V.tensor_tensor(fin, hT[:, :, CTX:NT],
                                 rms[:, 0:SEQ].unsqueeze(1).to_broadcast([P, KD, SEQ]), ALU.mult))
            V.tensor_tensor(fin, fin,
                            gains[:, 4, :].unsqueeze(2).to_broadcast([P, KD, SEQ]), ALU.mult).then_inc(out_ready, 1)

        @block.tensor
        def _(pe):
            mm = nc.tensor.matmul
            pe.wait_ge(inputs_in, 7 * 16)
            pe.wait_ge(l8_masked, 1)
            for k in range(2):
                last = nc.tensor.transpose(ps[:, k, 0:P], l8m[:, k].rearrange("p b s -> p (b s)"), ident)
            last.then_inc(l8_done, 1)
            pe.wait_ge(silu_c_ready, 1)
            pe.wait_ge(mod_bank_zero, 1)
            with pe.Fori(0, 2 * MB) as i:
                def turn(j):
                    pe.wait_ge(mod_rows_taken, i * RING + j + 1)
                    for q in range(4):
                        last = mm(ps[:, 4, 8 * j + 2 * q:8 * j + 2 * q + 2], mrow[:, j % 2, P * q:P * q + P],
                                  con[:, C_SEL:C_SEL + 2], start=True, stop=True)
                    last.then_inc(mod_cols_done, 1)
                for j in range(RING):
                    pe.wait_ge(landed[j], i * 16 + 16)
                    if j >= 2:
                        pe.wait_ge(mod_rows_taken, i * RING + j - 1)
                    wv = ring[j][:].rearrange("p (k c) -> p k c", k=KD)
                    for k in range(KD):
                        g = 32 * (k % 4)
                        last = mm(ps[g:g + 2, 6 + j % 2, :], silu_c[:, k, :], wv[:, k, :],
                                  start=(k < 4), stop=(k >= 4), skip_group_check=True)
                    last.then_inc(mod_rows_done, 1)
                    if j >= 1:
                        turn(j - 1)
                turn(RING - 1)
                pe.wait_ge(cp_masked, i * 2 + 2)
                pe.wait_ge(bp_masked, i * 2 + 2)
                cpv = CPm[:].rearrange("p a b k c s -> p (a b k) (c s)")
                bpv = BPm[:].rearrange("p a b k c s -> p (a b) k (c s)")
                for g in range(NK + 1):
                    if g >= 2:
                        pe.wait_ge(tr_taken, i * (NK + 1) + g - 1)
                    for j in range(4):
                        n = 4 * g + j
                        src = cpv[:, n, :] if n < 4 * NK else bpv[:, n - 4 * NK, 0, :]
                        last = nc.tensor.transpose(ps[:, g % 2, P * j:P * j + P], src, ident)
                    last.then_inc(tr_done, 1)
                pe.wait_ge(tr_taken, i * (NK + 1) + (NK + 1))
                for d in range(2):
                    for r in range(2):
                        o = (d * 2 + r) * NK
                        last = mm(ps[:, 2 + d, :], CTr[:, 4 * NK + d * 2 + r, :],
                                  CTr[:, o:o + CHUNK, :].rearrange("p a c -> p (a c)"), start=(r == 0), stop=(r == 1))
                last.then_inc(taps_done, 1)
                pe.wait_ge(kb_made, i + 1)
                pe.wait_ge(mod_cols_taken, i * RING + RING)

            def slot(key):
                n = stream_at[key]
                pe.wait_ge(landed[n % RING], 16 * (n // RING + 1))
                return ring[n % RING]

            def product(key, pairs, cols=NT, blocks=None):
                bank = bank_for(pe, key)
                for k, (w, x) in enumerate(pairs):
                    if blocks:
                        pe.wait_ge(blocks[0], blocks[1] + k + 1)
                    last = mm(bank[:, 0:cols], w, x, start=(k == 0), stop=(k == len(pairs) - 1))
                last.then_inc(place(key)[1], 1)

            def split_product(key, wh, wl, xh, xl, n, blocks, tile):
                bank = bank_for(pe, key)
                for k in range(n):
                    if blocks:
                        pe.wait_ge(a_high, k + 1)
                    mm(bank, wh[:, k, :], xh[:, k, :], start=(k == 0), stop=False)
                for k in range(n):
                    if blocks:
                        pe.wait_ge(blocks[0], blocks[1] + k + 1)
                    mm(bank, wh[:, k, :], xl[:, k, :], start=False, stop=False)
                pe.wait_ge(w_low, tile)
                for k in range(n):
                    last = mm(bank, wl[:, k, :], xh[:, k, :], start=False, stop=(k == n - 1))
                last.then_inc(place(key)[1], 1)

            def sums(l, n):
                lo = CTX if (l, n) == (1, 1) else 0
                bank = bank_for(pe, ("ss", l, n))
                for k in range(KD):
                    pe.wait_ge(sq_ready, KD * (2 * l + n) + k + 1)
                    last = mm(bank[:, lo:NT], ones, aT[:, k, lo:NT], start=(k == 0), stop=(k == KD - 1))
                last.then_inc(dense_done, 1)

            for l in range(DEPTH):
                t0 = CTX * l
                n_ = NT - t0
                sums(l, 0)
                w = slot(("w_in", l, 1))[:].rearrange("p (k c) -> p k c", k=KD)
                for m in range(4):
                    product(("u", l, m), [(w[:, k, P * m:P * m + P], aT[:, k, :]) for k in range(KD)],
                            blocks=(a_ready, KD * 2 * l) if m == 0 else None)
                for m in range(4):
                    taken(pe, ("u", l, m))
                    w = slot(("bp", l, m // 2))[:].rearrange("p (m d r k c) -> p m d r k c", m=2, d=2, r=2,
                                                             k=CHUNK)[:, m % 2]
                    uc = uT[:, m, :].rearrange("p (c j) -> p c j", j=CHUNK)
                    for g in range(4):
                        bank = bank_for(pe, ("E", l, m, g))
                        rows = slice(32 * g, 32 * g + 32)
                        for d in range(2):
                            for r in range(2):
                                o = (d * 2 + r) * NCH
                                for j in range(CHUNK):
                                    k = j if d else CHUNK - 1 - j
                                    last = mm(bank[:, o:o + NCH], w[rows, d, r, k, :], uc[rows, :, j],
                                              start=(j == 0), stop=(j == CHUNK - 1))
                        last.then_inc(side_done, 1)
                w = slot(("w_in", l, 0))[:].rearrange("p (k c) -> p k c", k=KD)
                for m in range(4):
                    product(("f", l, m), [(w[:, k, P * m:P * m + P], aT[:, k, t0:NT]) for k in range(KD)], n_)
                for m in range(4):
                    taken(pe, ("f", l, m))
                    for t in range(2 * l, 4):
                        product(("dft1", l, m, t), [(uF[:, m, P * t:P * t + P], con[:, C_CS:C_CS + 256])], 256)
                for m in range(4):
                    for s in range(l, 2):
                        pairs = []
                        for k in range(2):
                            t = 2 * s + k
                            taken(pe, ("dft1", l, m, t))
                            pairs += [(Q[:, t, m, 0:P], con[:, C_CN + 256 * k:C_CN + 256 * k + 256]),
                                      (Q[:, t, m, P:2 * P], con[:, C_SN + 256 * k:C_SN + 256 * k + 256])]
                        product(("dft2", l, m, s), pairs, 256)
                for name, tile in (("ga", 2), ("gb", 4)):
                    for h in range(2):
                        w = slot(("w_in", l, tile + h))[:].rearrange("p (k c) -> p k c", k=KD)
                        for m in range(4):
                            product((name, l, 4 * h + m),
                                    [(w[:, k, P * m:P * m + P], aT[:, k, t0:NT]) for k in range(KD)], n_)
                w = slot(("w_four", l, 0))[:].rearrange("p (k c) -> p k c", k=MB)
                for m in range(4):
                    taken(pe, ("dft2", l, m, 1))
                for m in range(8):
                    product(("ya", l, m), [(w[:, k, P * m:P * m + P], uF[:, k, t0:NT]) for k in range(MB)], n_)
                c0 = t0 // CHUNK
                for m in range(4):
                    bank = bank_for(pe, ("Y", l, m))
                    out_c = bank[:, 0:n_].rearrange("p (c j) -> p c j", j=CHUNK)
                    uc = uT[:, m, t0:NT].rearrange("p (c j) -> p c j", j=CHUNK)
                    tile = slot(("ck", l, m))
                    w = tile[:, CPW:CKW].rearrange("p (k c) -> p k c", k=2 * CHUNK - 1)
                    for k in range(CHUNK):
                        mm(out_c[:, :, k:CHUNK], w[:, k, :], uc[:, :, 0:CHUNK - k], start=(k == 0), stop=(k == 0), skip_group_check=True)
                        if k:
                            last = mm(out_c[:, :, 0:CHUNK - k], w[:, CHUNK + k % (CHUNK - 1), :], uc[:, :, k:CHUNK],
                                      start=False, stop=False, skip_group_check=True)
                    w = tile[:, 0:CPW].rearrange("p (d r k c) -> p d r k c", d=2, r=2, k=CHUNK)
                    if m == 0:
                        pe.wait_ge(scan_step, 4 * NCH * (l + 1))
                    for g in range(4):
                        rows = slice(32 * g, 32 * g + 32)
                        for r in range(2):
                            for j in range(CHUNK):
                                col = m * 8 + g
                                mm(out_c[rows, :, j], w[:, 0, r, j, rows], H[:, c0:NCH, r, col],
                                   start=False, stop=False, skip_group_check=True)
                                hv = H[:, 0:NCH, r, col + 4].rearrange("p (s c) -> p s c", s=2)[:, l:2, ::-1]
                                last = mm(out_c[rows, :, j].rearrange("p (s c) -> p s c", s=2 - l),
                                          w[:, 1, r, CHUNK - 1 - j, rows], hv,
                                          start=False, stop=(g == 3 and r == 1 and j == CHUNK - 1), skip_group_check=True)
                    last.then_inc(side_done, 1)
                for name in ("glub", "glua"):
                    w = slot(("w_" + name[:3] + "_" + name[3], l, 0))[:].rearrange("p (k c) -> p k c", k=MB)
                    pe.wait_ge(ys_ready, 4 * l + 4)
                    for m in range(8):
                        product((name, l, m), [(w[:, k, P * m:P * m + P], ysT[:, k, t0:NT]) for k in range(MB)], n_)
                pe.wait_ge(mix_ready, 8 * l + 8)
                for h in range(2):
                    w = slot(("w_out", l, h))[:].rearrange("p (k c) -> p k c", k=KD)
                    for m in range(4):
                        product(("out", l, 4 * h + m),
                                [(w[:, k, P * m:P * m + P], G[:, k, t0:NT]) for k in range(KD)], n_)
                sums(l, 1)
                if l == 1:
                    pe.wait_ge(a_ready, 4 * KD)
                if l == 0:
                    for i_, (name, _, t) in enumerate(ffn_tiles):
                        pe.wait_ge(w_high, i_ + 1)
                        part = int(name[-1]) if name[-1] in "01" else None
                        w_ = tile_src(ffn_tiles[i_]).shape[-1]
                        low = ringl[stream_at[ffn_tiles[i_]] % RING][:, 0:w_]
                        if part is None:
                            wh, wl = (v.rearrange("p (u k c) -> p u k c", u=2, k=KD) for v in (FWH[i_ % 2][:], low))
                            for m in range(2):
                                for u, n_u in enumerate(("gate", "up")):
                                    split_product((n_u, l, 2 * t + m), wh[:, u, :, P * m:P * m + P],
                                                  wl[:, u, :, P * m:P * m + P], aTh, aTl, KD,
                                                  (a_ready, KD) if i_ + m + u == 0 else None, i_ + 1)
                        else:
                            if t == 0:
                                pe.wait_ge(hid_low, sum(PARTS[:part + 1]))
                            wh, wl = (v.rearrange("p (k c) -> p k c", k=PARTS[part])
                                      for v in (FWH[i_ % 2][:, 0:w_], low))
                            for m in range(2):
                                split_product((name[4:], l, 2 * t + m), wh[:, :, P * m:P * m + P],
                                              wl[:, :, P * m:P * m + P], hidh, hidl, PARTS[part],
                                              None, i_ + 1)

            for t in range(2):
                for k in range(KD):
                    last = mm(ps[:, 7, NE * t:NE * t + NE], aT[:, k, CTX + P * t:CTX + P * t + P], wrt[:, k, :],
                              start=(k == 0), stop=(k == KD - 1))
            last.then_inc(logits_done, 1)
            for g in range(4):
                for j in range(4):
                    k = 4 * (g % 2) + j
                    last = nc.tensor.transpose(ps[:, g, P * j:P * j + P],
                                               aT[:, k, CTX + P * (g // 2):CTX + P * (g // 2) + P], ident)
                last.then_inc(ftok_done, 1)
            pe.wait_ge(sel_ready, 1)
            tri = con[:, C_TRI:C_TRI + P]
            mm(ps[:, 7, 16:24], tri, sel[:, 0, :], start=True, stop=True)
            mm(ps[:, 7, 24:32], ones, sel[:, 0, :], start=True, stop=False)
            mm(ps[:, 7, 24:32], tri, sel[:, 1, :], start=False, stop=True)
            mm(ps[:, 7, 32:40], ones, sel[:, 0, :], start=True, stop=False)
            mm(ps[:, 7, 32:40], ones, sel[:, 1, :], start=False, stop=True).then_inc(rank_done, 1)
            pe.wait_ge(ftok_ready, 4)
            pe.wait_ge(count_ready, 1)

            def misc(pas, e, what):
                b, n, _ = misc_use(pas, e, what)
                if not isinstance(e, str) or e != "before" or pas or what[0] == "W":
                    pe.wait_ge(misc_taken[b], n)
                return ps[:, 6 + b, :]

            def gather(pas, e, g):
                bank = misc(pas, e, ("G", g))
                for k in range(4):
                    for t in range(2):
                        o = P * (4 * g + k)
                        last = mm(bank[:, P * k:P * k + P], ftok[:, t, o:o + P], S[:, t, :],
                                  start=(t == 0), stop=(t == 1))
                last.then_inc(misc_done, 1)

            def turn_weights(pas, e):
                bank = misc(pas, e, ("W", 0))
                for t in range(2):
                    last = nc.tensor.transpose(bank[:, P * t:P * t + P], SW[:, t, :], ident)
                last.then_inc(misc_done, 1)

            def turn_hidden(pas, e, x, c):
                bank = misc(pas, e, ("T", c))
                pe.wait_ge(hid_ready, x * FCH + c + 1)
                for j in range(4):
                    last = nc.tensor.transpose(bank[:, P * j:P * j + P], hd[:, c % 2, P * j:P * j + P], ident)
                last.then_inc(misc_done, 1)

            def scatter(pas, e, j, par):
                bank = misc(pas, e, ("S", j))
                for i_ in range(2):
                    m = 2 * j + i_
                    last = mm(bank[:, 256 * i_:256 * i_ + 256], ye[:, P * m:P * m + P], SWT[:, par, :],
                              start=True, stop=True)
                last.then_inc(misc_done, 1)

            def experts(pas):
                pe.wait_ge(onehot_ready, (NE + 1) * pas + 1)
                for g in range(2):
                    gather(pas, "before", g)
                turn_weights(pas, "before")
                pe.wait_ge(scatter_zero, pas + 1)
                for g in range(2):
                    b, n, _ = misc_use(pas, "before", ("G", g))
                    pe.wait_ge(misc_taken[b], n + 1)
                with pe.Fori(0, NE // 2) as i:
                    for par in range(2):
                        e = i * 2 + par
                        x = e + NE * pas
                        for t, (kind, c) in enumerate(moe_order):
                            buf = (par + t) % 2
                            high = x * (2 * TILES) + 2 * t
                            if kind == "down":
                                outs = [(ps[:, 4 + h, :],
                                         [((hTh[:, c % 2, j, :], hTl[:, c % 2, j, :]), D * j + 512 * h)
                                          for j in range(4)], c == 0, c == FCH - 1) for h in range(2)]
                                b, n, _ = misc_use(pas, e, ("T", c))
                                pe.wait_ge(misc_taken[b], n + 1)
                            else:
                                outs = [(ps[:, 2 * (c % 2) + (kind == "up"), :],
                                         [((XGh[:, k, :], XGl[:, k, :]), 512 * k) for k in range(KD)], True, True)]
                                if kind == "gate" and c >= 2:
                                    pe.wait_ge(hid_ready, x * FCH + c - 1)
                                if kind == "gate" and c == 0 and par:
                                    for g in range(2):
                                        b, n, _ = misc_use(pas, e - 1, ("G", g))
                                        pe.wait_ge(misc_taken[b], n + 1)
                            seen = 0
                            for out_, pairs, first, final in outs:
                                for q, ((ah, al), o) in enumerate(pairs):
                                    half = 1 if kind == "down" and q < 2 else 2 if kind == "down" else 1 + (q >= 4)
                                    if half > seen:
                                        pe.wait_ge(high_done, high + half)
                                        seen = half
                                    mm(out_, ah, WH[buf][:, o:o + 512], start=(first and q == 0), stop=False)
                                    mm(out_, al, WH[buf][:, o:o + 512], start=False, stop=False)
                            seen = 0
                            for out_, pairs, first, final in outs:
                                for q, ((ah, al), o) in enumerate(pairs):
                                    half = 1 if kind == "down" and q < 2 else 2 if kind == "down" else 1 + (q >= 4)
                                    if half > seen:
                                        pe.wait_ge(low_done, high + half)
                                        seen = half
                                    last = mm(out_, ah, WL[buf][:, o:o + 512], start=False,
                                              stop=(final and q == len(pairs) - 1))
                            last.then_inc(tile_done, 1)
                            if kind == "gate":
                                if c == 0:
                                    pe.wait_ge(ye_ready, x * 2 + 2)
                                    for j in range(2):
                                        scatter(pas, e, j, 1 - par)
                                else:
                                    turn_hidden(pas, e, x, c - 1)
                            if (kind, c) == ("up", 0):
                                for j in range(2, 4):
                                    scatter(pas, e, j, 1 - par)
                            if (kind, c) == ("up", 5):
                                pe.wait_ge(onehot_ready, x + 2 + pas)
                                turn_weights(pas, e)
                            if (kind, c) == ("up", 6):
                                for g in range(2):
                                    gather(pas, e, g)
                                turn_hidden(pas, e, x, 6)
                    for g in range(2):
                        b, n, _ = misc_use(pas, e, ("G", g))
                        pe.wait_ge(misc_taken[b], n + 1)
                pe.wait_ge(ye_ready, 2 * NE * (pas + 1) + 2)
                for j in range(4):
                    scatter(pas, "after", j, 1)
            experts(0)
            most = pe.value_load(cnti[0:1, 0:1], min_val=0, max_val=SEQ)
            with pe.If(most > P):
                experts(1)
            pe.wait_ge(sq_ready, 2 * DEPTH * KD + 1)
            for k in range(KD):
                last = mm(ps[:, 0, 0:SEQ], ones, fin[:, k, :], start=(k == 0), stop=(k == KD - 1))
            last.then_inc(fin_done, 1)


def layout(x, c, ctx, c_ctx, w_mod, b_mod, norm1_g, norm2_g, w_in, w_four, ssm_a_re, ssm_a_im, ssm_log_dt,
           ssm_b_re, ssm_b_im, ssm_c_re, ssm_c_im, ssm_d, w_glu_a, w_glu_b, w_out, ffn_w_gate, ffn_w_up,
           ffn_w_down, moe_w_router, moe_b_router, moe_w_gate, moe_w_up, moe_w_down, final_g):
    def cut(w, rows, cols):
        lead = w.shape[:-2]
        k, n = w.shape[-2:]
        w = w.reshape(*lead, k // P, P, n // cols, cols)
        nl = len(lead)
        w = w.transpose(*range(nl), nl + 2, nl + 1, nl, nl + 3)
        return w.reshape(*lead, n // cols, P, (k // P) * cols)

    def vec(v):
        v = v.reshape(*v.shape[:-1], v.shape[-1] // P, P)
        return np.moveaxis(v, -1, 0)

    def rows(v):
        v = v.reshape(DEPTH, 2, MB, 8, *v.shape[3:])
        return v.swapaxes(1, 2)

    r = {"con": constants(), "pos": positions()}
    tok = np.concatenate([ctx[0], x[0]], axis=0)
    r["xT"] = tok.T.reshape(KD, P, NT).transpose(1, 0, 2)
    r["cT"] = np.stack([vec(c_ctx), vec(c[0])], axis=-1)
    r["w_mod"] = cut(w_mod, D, 512).reshape(ADA_TILES, P, SLOT)
    r["bmod"] = vec(b_mod)
    r["gains"] = vec(np.stack([norm1_g[0], norm2_g[0], norm1_g[1], norm2_g[1], final_g]))
    r["w_in"] = cut(w_in, D, 512)
    r["w_out"] = cut(w_out, D, 512)
    for n, w in (("w_four", w_four), ("w_glu_a", w_glu_a), ("w_glu_b", w_glu_b)):
        r[n] = cut(w, WF, D)[:, 0]
    r["lam"] = np.stack([rows(ssm_a_re), rows(ssm_a_im)], axis=-2).reshape(P, 2, ST)
    r["ldt"] = rows(ssm_log_dt).reshape(P, 1)
    b = np.stack([rows(ssm_b_re), rows(ssm_b_im)], axis=3).transpose(0, 1, 4, 6, 2, 3, 5)
    cc = np.stack([rows(ssm_c_re), rows(ssm_c_im)], axis=3).transpose(0, 1, 4, 5, 2, 3, 6)
    r["bc"] = np.stack([b, cc], axis=4).reshape(2 * MB, P, 2 * 2 * 2 * ST)
    r["dskip"] = vec(ssm_d)
    g = cut(ffn_w_gate[0], D, 256)
    u = cut(ffn_w_up[0], D, 256)
    r["ffn_gu"] = np.concatenate([g, u], axis=-1)
    r["ffn_down0"] = cut(ffn_w_down[0, :PARTS[0] * P], PARTS[0] * P, 256)
    r["ffn_down1"] = cut(ffn_w_down[0, PARTS[0] * P:], PARTS[1] * P, 256)
    r["wrt"] = moe_w_router[0].reshape(KD, P, NE).transpose(1, 0, 2)
    r["brt"] = np.broadcast_to(moe_b_router[0], (P, NE))
    r["moe_gate"] = cut(moe_w_gate[0], D, 512).reshape(NE * FCH, P, SLOT)
    r["moe_up"] = cut(moe_w_up[0], D, 512).reshape(NE * FCH, P, SLOT)
    r["moe_down"] = moe_w_down[0].reshape(NE, FCH, 4, P, D).transpose(0, 1, 3, 2, 4).reshape(NE * FCH, P, SLOT)
    return {k: np.ascontiguousarray(v) for k, v in r.items()}


def declare(nc, arrays):
    a = {k: nc.dram_tensor("in_" + k, v.shape, F32, kind="ExternalInput").ap() for k, v in arrays.items()}
    out = nc.dram_tensor("out", (P, KD, SEQ), F32, kind="ExternalOutput").ap()
    tab = nc.dram_tensor("tab", (P, TAB), F32, kind="Internal").ap()
    bps = nc.dram_tensor("bps", (2 * MB, P, 8 * CHUNK * ST), F32, kind="Internal").ap()
    cks = nc.dram_tensor("cks", (2 * MB, P, CKW), F32, kind="Internal").ap()
    program(nc, a, out, tab, bps, cks)


def kernel(**inputs):
    import concourse.bacc as bacc
    from concourse.bass_utils import run_bass_kernel_spmd

    arrays = layout(**{k: np.asarray(v) for k, v in inputs.items()})
    nc = bacc.Bacc("TRN2", target_bir_lowering=False, num_devices=1)
    declare(nc, arrays)
    r = run_bass_kernel_spmd(nc, [{"in_" + k: v for k, v in arrays.items()}], core_ids=[0])
    y = r.results[0]["out"]
    return np.ascontiguousarray(y.transpose(1, 0, 2).reshape(D, SEQ).T)[None]
```
